# Optimizing a Trainium2 kernel written in Bass

```python
import jax, jax.numpy as jnp
from jax import lax
import numpy as np

D_MODEL = 1024
BATCH = 1
SEQ = 256
DEPTH = 2
DEC_BATCH = 8
DEC_SEQ = 4
PAST_LEN = 2048
PAGE_SIZE = 128

HEAD_DIM = 64
MIX_WIDTH = D_MODEL
A_GROUPS = ((128, 1), (512, 4), (2048, 16))
A_HEADS_PER_GROUP = 2
A_HEADS = A_HEADS_PER_GROUP * len(A_GROUPS)
A_WIDTH = A_HEADS * HEAD_DIM
B_WIDTH = (MIX_WIDTH - A_WIDTH) // 2
C_WIDTH = MIX_WIDTH - A_WIDTH - B_WIDTH
C_HEADS = C_WIDTH // HEAD_DIM
CONV_WIDTH = 3
CHUNK = 128
BAND_BLOCK = 128
N_BUCKETS = 32
REL_MAX_DIST = 2048
PEER_HEADS = 8
N_KEYS = 128
N_EXPERTS = N_KEYS * N_KEYS
D_KEY = 256
TOPK_HALF = 16
TOPK = 16
PEER_BLOCK = 256
EPS = 1e-6
NEG = -1e30
SCALE = HEAD_DIM ** -0.5
IN_COLS = 3 * A_WIDTH + 3 * B_WIDTH + 2 * C_WIDTH
IN_SPLITS = (A_WIDTH, 2 * A_WIDTH, 3 * A_WIDTH, 3 * A_WIDTH + B_WIDTH, 3 * A_WIDTH + 2 * B_WIDTH,
             3 * A_WIDTH + 3 * B_WIDTH, 3 * A_WIDTH + 3 * B_WIDTH + C_WIDTH)

kernel_name = 'hymba_dilated_conv_gmlp_peer_step'

def _rms(x, g):
    xf = x.astype(jnp.float32)
    y = xf * lax.rsqrt(jnp.mean(xf * xf, axis=-1, keepdims=True) + EPS)
    return (y * g.astype(jnp.float32)).astype(x.dtype)

def _t5_bucket(dist):
    d = np.maximum(np.asarray(dist), 0)
    max_exact = N_BUCKETS // 2
    ratio = np.log(np.maximum(d, 1).astype(np.float32) / max_exact) / np.log(REL_MAX_DIST / max_exact)
    large = np.minimum(max_exact + (ratio * (N_BUCKETS - max_exact)).astype(np.int32), N_BUCKETS - 1)
    return np.where(d < max_exact, d, large).astype(np.int32)

def _mixer_front(xn, w_in, q_g, k_g, cv_g):
    shp = xn.shape[:-1]
    qa, ka, va, xb, gb, gc, cu, cv = jnp.split(xn @ w_in, IN_SPLITS, axis=-1)
    q = _rms(qa.reshape(*shp, A_HEADS, HEAD_DIM), q_g)
    k = _rms(ka.reshape(*shp, A_HEADS, HEAD_DIM), k_g)
    v = va.reshape(*shp, A_HEADS, HEAD_DIM)
    zb = gc * xb
    u = jax.nn.gelu(cu).reshape(*shp, C_HEADS, HEAD_DIM)
    vc = _rms(jax.nn.gelu(cv).reshape(*shp, C_HEADS, HEAD_DIM), cv_g)
    return q, k, v, zb, gb, u, vc

def _dilated_band_prompt(q, k, v, bias_tab, window, dil):
    b, s, h, dh = q.shape
    n_off = window // dil
    L = s // dil
    nb = -(-L // BAND_BLOCK)
    Lp = nb * BAND_BLOCK
    bp = b * dil

    def to_sub(t):
        t = t.reshape(b, L, dil, h, dh).transpose(0, 2, 1, 3, 4).reshape(bp, L, h, dh)
        return jnp.pad(t, ((0, 0), (0, Lp - L), (0, 0), (0, 0)))

    def two_blocks(t):
        prev = jnp.pad(t, ((0, 0), (BAND_BLOCK, 0), (0, 0), (0, 0)))[:, :Lp].reshape(bp, nb, BAND_BLOCK, h, dh)
        return jnp.concatenate([prev, t.reshape(bp, nb, BAND_BLOCK, h, dh)], axis=2)

    qb = to_sub(q).reshape(bp, nb, BAND_BLOCK, h, dh)
    kb = two_blocks(to_sub(k))
    vb = two_blocks(to_sub(v))
    qi = np.arange(BAND_BLOCK)[:, None]
    kj = np.arange(2 * BAND_BLOCK)[None, :]
    off = qi + BAND_BLOCK - kj
    band = (off >= 0) & (off <= n_off)
    mask = band[None] & ((np.arange(nb)[:, None, None] > 0) | (kj[None] >= BAND_BLOCK))
    bias = jnp.take(bias_tab, _t5_bucket(off * dil), axis=0).transpose(2, 0, 1).astype(jnp.float32)
    logits = jnp.einsum('bnqhd,bnkhd->bnhqk', qb, kb).astype(jnp.float32) * SCALE + bias
    logits = jnp.where(mask[None, :, None], logits, NEG)
    lse = jax.nn.logsumexp(logits, axis=-1)
    p = jnp.exp(logits - lse[..., None])
    o = jnp.einsum('bnhqk,bnkhd->bnqhd', p.astype(v.dtype), vb)
    o = o.reshape(b, dil, Lp, h, dh)[:, :, :L].transpose(0, 2, 1, 3, 4).reshape(b, s, h, dh)
    lse = lse.transpose(0, 1, 3, 2).reshape(b, dil, Lp, h)[:, :, :L].transpose(0, 2, 1, 3).reshape(b, s, h)
    return o, lse

def _dilated_gather_sample(q, kv_new, kv_buf, bias_tab, window, dil):
    t = q.shape[1]
    lb = kv_buf.shape[1]
    n_off = window // dil
    kv_all = jnp.concatenate([kv_buf, kv_new], axis=1)
    jj = np.arange(n_off + 1)
    idx = lb + np.arange(t)[:, None] - jj[None, :] * dil
    valid = idx >= 0
    g = kv_all[:, np.maximum(idx, 0)]
    bias = jnp.take(bias_tab, _t5_bucket(jj * dil), axis=0).T.astype(jnp.float32)
    logits = jnp.einsum('bthd,btkhd->bthk', q, g[:, :, :, 0]).astype(jnp.float32) * SCALE + bias[None, None]
    logits = jnp.where(valid[None, :, None, :], logits, NEG)
    lse = jax.nn.logsumexp(logits, axis=-1)
    p = jnp.exp(logits - lse[..., None])
    o = jnp.einsum('bthk,btkhd->bthd', p.astype(q.dtype), g[:, :, :, 1])
    return o, lse, kv_all[:, -lb:]

def _combine_groups(outs, lses):
    alpha = jax.nn.softmax(jnp.stack(lses, axis=0), axis=0)
    a = jnp.concatenate([o * alpha[i][..., None].astype(o.dtype) for i, o in enumerate(outs)], axis=-2)
    return a.reshape(*a.shape[:-2], A_WIDTH)

def _conv3(zz, w, t):
    y = w[0] * zz[:, :t]
    for j in range(1, CONV_WIDTH):
        y = y + w[j] * zz[:, j:j + t]
    return y

def _chunk_mlp_prompt(u, vc, ws, bs):
    b, s = u.shape[:2]
    wm = jnp.where(np.tril(np.ones((CHUNK, CHUNK), bool)), ws, 0)
    vr = vc.reshape(b, s // CHUNK, CHUNK, C_HEADS, HEAD_DIM)
    mix = jnp.einsum('hts,bnshd->bnthd', wm, vr) + bs.T[:, :, None]
    return u * mix.reshape(b, s, C_HEADS, HEAD_DIM)

def _chunk_mlp_sample(u, vc, ws, bs):
    t = u.shape[1]
    wm = jnp.where(np.tril(np.ones((t, t), bool)), ws[:, :t, :t], 0)
    return u * (jnp.einsum('hts,bshd->bthd', wm, vc) + bs[:, :t].T[:, :, None])

def _merge_out(ya, yb, yc, w_out):
    yc = yc.reshape(*yc.shape[:-2], C_WIDTH)
    return jnp.concatenate([ya, yb, yc], axis=-1) @ w_out

def _peer(xn, wq, k1, k2, eu, ev):
    shp = xn.shape
    xt = xn.reshape(-1, shp[-1])
    n = xt.shape[0]
    blk = min(PEER_BLOCK, n)
    nblk = -(-n // blk)
    xt = jnp.pad(xt, ((0, nblk * blk - n), (0, 0))).reshape(nblk, blk, shp[-1])

    def one_block(xb):
        q = (xb @ wq).reshape(blk, PEER_HEADS, 2, D_KEY // 2)
        s1 = jnp.einsum('nhd,kd->nhk', q[:, :, 0], k1).astype(jnp.float32)
        s2 = jnp.einsum('nhd,kd->nhk', q[:, :, 1], k2).astype(jnp.float32)
        t1, i1 = lax.top_k(s1, TOPK_HALF)
        t2, i2 = lax.top_k(s2, TOPK_HALF)
        cand = (t1[..., :, None] + t2[..., None, :]).reshape(blk, PEER_HEADS, TOPK_HALF * TOPK_HALF)
        ts, ti = lax.top_k(cand, TOPK)
        e = (jnp.take_along_axis(i1, ti // TOPK_HALF, axis=-1) * N_KEYS
             + jnp.take_along_axis(i2, ti % TOPK_HALF, axis=-1))
        g = jax.nn.softmax(ts, axis=-1)
        hid = jax.nn.gelu(jnp.einsum('nd,nhkd->nhk', xb, eu[e]))
        return jnp.einsum('nhk,nhkd->nd', (g * hid).astype(xb.dtype), ev[e])

    y = lax.map(one_block, xt)
    return y.reshape(nblk * blk, shp[-1])[:n].reshape(shp)

def _layer_prompt(x, rel_bias, lp):
    (g_mix, w_in, q_g, k_g, conv_w, cv_g, c_ws, c_bs, w_out, g_ffn, pq, pk1, pk2, pu, pv) = lp
    s = x.shape[1]
    q, k, v, zb, gb, u, vc = _mixer_front(_rms(x, g_mix), w_in, q_g, k_g, cv_g)
    outs, lses, kv_rows = [], [], []
    for i, (win, dil) in enumerate(A_GROUPS):
        sl = slice(i * A_HEADS_PER_GROUP, (i + 1) * A_HEADS_PER_GROUP)
        o, lse = _dilated_band_prompt(q[:, :, sl], k[:, :, sl], v[:, :, sl], rel_bias[:, sl], win, dil)
        outs.append(o)
        lses.append(lse)
        kv_rows.append(jnp.stack([k[:, :, sl], v[:, :, sl]], axis=2)[:, s - min(win, s):])
    ya = _combine_groups(outs, lses)
    zz = jnp.pad(zb, ((0, 0), (CONV_WIDTH - 1, 0), (0, 0)))
    yb = gb * _conv3(zz, conv_w, s)
    conv_rows = zz[:, -(CONV_WIDTH - 1):]
    yc = _chunk_mlp_prompt(u, vc, c_ws, c_bs)
    h = x + _merge_out(ya, yb, yc, w_out)
    y = h + _peer(_rms(h, g_ffn), pq, pk1, pk2, pu, pv)
    return y, kv_rows, conv_rows

def _layer_sample(x, kv_bufs, conv_buf, rel_bias, lp):
    (g_mix, w_in, q_g, k_g, conv_w, cv_g, c_ws, c_bs, w_out, g_ffn, pq, pk1, pk2, pu, pv) = lp
    t = x.shape[1]
    q, k, v, zb, gb, u, vc = _mixer_front(_rms(x, g_mix), w_in, q_g, k_g, cv_g)
    kv_new = jnp.stack([k, v], axis=2)
    outs, lses, new_bufs = [], [], []
    for i, (win, dil) in enumerate(A_GROUPS):
        sl = slice(i * A_HEADS_PER_GROUP, (i + 1) * A_HEADS_PER_GROUP)
        o, lse, nbuf = _dilated_gather_sample(q[:, :, sl], kv_new[:, :, :, sl], kv_bufs[i], rel_bias[:, sl], win, dil)
        outs.append(o)
        lses.append(lse)
        new_bufs.append(nbuf)
    ya = _combine_groups(outs, lses)
    zz = jnp.concatenate([conv_buf, zb], axis=1)
    yb = gb * _conv3(zz, conv_w, t)
    new_conv = zz[:, -(CONV_WIDTH - 1):]
    yc = _chunk_mlp_sample(u, vc, c_ws, c_bs)
    h = x + _merge_out(ya, yb, yc, w_out)
    y = h + _peer(_rms(h, g_ffn), pq, pk1, pk2, pu, pv)
    return y, new_bufs, new_conv, vc

def setup_inputs(seed: int = 0) -> dict:
    key = jax.random.key(seed)
    ks = jax.random.split(key, 24)
    f32 = jnp.float32

    def nrm(k, shape, scale):
        return jax.random.normal(k, shape, f32) * scale

    return {
        'x_prompt': nrm(ks[0], (BATCH, SEQ, D_MODEL), 1.0),
        'x_sample': nrm(ks[1], (DEC_BATCH, DEC_SEQ, D_MODEL), 1.0),
        'cache_a_kv_w128': nrm(ks[2], (DEPTH, DEC_BATCH, min(A_GROUPS[0][0], PAST_LEN), 2, A_HEADS_PER_GROUP, HEAD_DIM), 1.0),
        'cache_a_kv_w512': nrm(ks[3], (DEPTH, DEC_BATCH, min(A_GROUPS[1][0], PAST_LEN), 2, A_HEADS_PER_GROUP, HEAD_DIM), 1.0),
        'cache_a_kv_w2048': nrm(ks[4], (DEPTH, DEC_BATCH, min(A_GROUPS[2][0], PAST_LEN), 2, A_HEADS_PER_GROUP, HEAD_DIM), 1.0),
        'state_b_conv': nrm(ks[5], (DEPTH, DEC_BATCH, CONV_WIDTH - 1, B_WIDTH), 1.0),
        'rel_bias': nrm(ks[6], (N_BUCKETS, A_HEADS), 0.5),
        'norm_mix': 1.0 + nrm(ks[7], (DEPTH, D_MODEL), 0.05),
        'w_in': nrm(ks[8], (DEPTH, D_MODEL, IN_COLS), D_MODEL ** -0.5),
        'q_norm': 1.0 + nrm(ks[9], (DEPTH, HEAD_DIM), 0.05),
        'k_norm': 1.0 + nrm(ks[10], (DEPTH, HEAD_DIM), 0.05),
        'conv_w': nrm(ks[11], (DEPTH, CONV_WIDTH, B_WIDTH), CONV_WIDTH ** -0.5),
        'c_v_norm': 1.0 + nrm(ks[12], (DEPTH, C_HEADS, HEAD_DIM), 0.05),
        'c_ws': nrm(ks[13], (DEPTH, C_HEADS, CHUNK, CHUNK), CHUNK ** -0.5),
        'c_bs': 1.0 + nrm(ks[14], (DEPTH, C_HEADS, CHUNK), 0.1),
        'w_out': nrm(ks[15], (DEPTH, MIX_WIDTH, D_MODEL), MIX_WIDTH ** -0.5),
        'norm_ffn': 1.0 + nrm(ks[16], (DEPTH, D_MODEL), 0.05),
        'peer_wq': nrm(ks[17], (DEPTH, D_MODEL, PEER_HEADS * D_KEY), D_MODEL ** -0.5),
        'peer_k1': nrm(ks[18], (DEPTH, N_KEYS, D_KEY // 2), (D_KEY // 2) ** -0.5),
        'peer_k2': nrm(ks[19], (DEPTH, N_KEYS, D_KEY // 2), (D_KEY // 2) ** -0.5),
        'peer_u': nrm(ks[20], (DEPTH, N_EXPERTS, D_MODEL), D_MODEL ** -0.5),
        'peer_v': nrm(ks[21], (DEPTH, N_EXPERTS, D_MODEL), 0.25),
    }

def reference(x_prompt, x_sample, cache_a_kv_w128, cache_a_kv_w512, cache_a_kv_w2048, state_b_conv,
              rel_bias, norm_mix, w_in, q_norm, k_norm, conv_w, c_v_norm, c_ws, c_bs, w_out, norm_ffn,
              peer_wq, peer_k1, peer_k2, peer_u, peer_v):
    yp, ys = x_prompt, x_sample
    kvp = [[], [], []]
    kvs = [[], [], []]
    convp, convs, cvs = [], [], []
    for l in range(DEPTH):
        lp = (norm_mix[l], w_in[l], q_norm[l], k_norm[l], conv_w[l], c_v_norm[l], c_ws[l], c_bs[l],
              w_out[l], norm_ffn[l], peer_wq[l], peer_k1[l], peer_k2[l], peer_u[l], peer_v[l])
        yp, rows, crow = _layer_prompt(yp, rel_bias, lp)
        ys, bufs, cbuf, vrows = _layer_sample(
            ys, (cache_a_kv_w128[l], cache_a_kv_w512[l], cache_a_kv_w2048[l]), state_b_conv[l], rel_bias, lp)
        for i in range(len(A_GROUPS)):
            kvp[i].append(rows[i])
            kvs[i].append(bufs[i])
        convp.append(crow)
        convs.append(cbuf)
        cvs.append(vrows)
    return (yp, ys,
            jnp.stack(kvp[0]), jnp.stack(kvs[0]),
            jnp.stack(kvp[1]), jnp.stack(kvs[1]),
            jnp.stack(kvp[2]), jnp.stack(kvs[2]),
            jnp.stack(convp), jnp.stack(convs),
            jnp.stack(cvs))


_drawn_inputs = setup_inputs


def setup_inputs(seed=0):
    import zlib

    import numpy as np

    out = dict(_drawn_inputs(seed))
    spreads = {}
    factors = {'q_norm': 5.394}
    for name, (base, spread) in spreads.items():
        noise = np.random.default_rng([zlib.crc32(name.encode()), seed]).standard_normal(out[name].shape)
        drawn = base * np.exp(spread * noise) if base else spread * noise
        out[name] = __import__('jax').numpy.asarray(drawn.astype(out[name].dtype))
    for name, factor in factors.items():
        out[name] = (out[name] * factor).astype(out[name].dtype)
    return out
```

```python
from contextlib import ExitStack

import numpy as np

import concourse.bass as bass
from concourse import mybir

F32 = mybir.dt.float32
U32 = mybir.dt.uint32
ACT = mybir.ActivationFunctionType
ALU = mybir.AluOpType
AX = mybir.AxisListType

P = 128
D = 1024
DEPTH = 2
SEQ = 256
NB, NT = 8, 4
NS = NB * NT
TOKENS = SEQ + NS
TILES = 3
ROWS = (P, P, NS)
T0 = (0, P, 2 * P)
HD = 64
GROUPS = ((128, 1), (512, 4), (2048, 16))
NG = len(GROUPS)
HEADS = 2 * NG
AW = HEADS * HD
BW = (D - AW) // 2
CW = D - AW - BW
CH = CW // HD
IN_COLS = 3 * AW + 3 * BW + 2 * CW
Q0, K0, V0 = 0, AW, 2 * AW
XB0, GB0, GC0 = 3 * AW, 3 * AW + BW, 3 * AW + 2 * BW
U0 = 3 * AW + 3 * BW
CV0 = U0 + CW
KCH = D // P
N_IN, W_IN = 8, IN_COLS // 8
N_OUT, W_OUT = 4, 256
N_Q, W_Q = 8, 256
N_W = N_IN + N_OUT + N_Q
SLOT = KCH * W_IN
N_BUCKETS = 32
REL_MAX = 2048
NEG = -1e30
EPS = 1e-6
SCALE = HD ** -0.5
PH = 8
NK = 128
NE = NK * NK
TOP = 16
PICKS = PH * TOP
BATCH = 8
BATCHES = (PICKS // BATCH, PICKS // BATCH, PICKS // BATCH // 4)
BASE = (0, BATCHES[0], 2 * BATCHES[0])
ALL_B = sum(BATCHES)
COL0 = (0, PICKS, 2 * PICKS)
PITCH = 384
LOW = -3.0e38


def bucket(dist):
    d = np.maximum(np.asarray(dist), 0)
    half = N_BUCKETS // 2
    ratio = np.log(np.maximum(d, 1).astype(np.float32) / half) / np.log(REL_MAX / half)
    large = np.minimum(half + (ratio * (N_BUCKETS - half)).astype(np.int32), N_BUCKETS - 1)
    return np.where(d < half, d, large).astype(np.int32)


def shape_constants():
    prompt = np.zeros((N_BUCKETS + 1, NG, PITCH), np.float32)
    for g, (win, dil) in enumerate(GROUPS):
        for u in range(PITCH - 1):
            d = 255 - u
            if 0 <= d <= win and d % dil == 0:
                prompt[bucket(d), g, u] = 1
            else:
                prompt[N_BUCKETS, g, u] = NEG
    sample = np.zeros((N_BUCKETS + 1, NG, NT, P + NS), np.float32)
    for g, (win, dil) in enumerate(GROUPS):
        for t in range(NT):
            for m in range(P):
                d = P + t - m if g == 0 else win - dil * m
                if d <= win:
                    sample[bucket(d), g, t, m] = 1
                else:
                    sample[N_BUCKETS, g, t, m] = NEG
            for n in range(NS):
                d = t - n % NT
                if d == 0 or (g == 0 and d > 0):
                    sample[bucket(d), g, t, P + n] = 1
                else:
                    sample[N_BUCKETS, g, t, P + n] = NEG
    turn = np.zeros((N_BUCKETS + 1, NT, NS), np.float32)
    for t in range(NT):
        turn[:, t, t::NT] = 1
    other = np.zeros((NS, P + NS), np.float32)
    for n in range(NS):
        for k in range(NS):
            if n // NT != k // NT:
                other[n, P + k] = NEG
    ident = np.zeros((P, 2, P), np.float32)
    ident[:, 0] = np.eye(P)
    for p in range(P):
        ident[p, 1, p % NS] = 1
    sixteen = np.tile(np.arange(TOP, dtype=np.float32), (P, 1))
    return {
        "c_prompt": prompt, "c_sample": sample.reshape(N_BUCKETS + 1, -1), "c_turn": turn.reshape(N_BUCKETS + 1, -1),
        "c_other": other, "c_ident": ident.reshape(P, -1), "c_sixteen": sixteen,
    }


def trunk(nc, io):
    ctx = ExitStack()
    with ctx:
        def sb(name, shape, dt=F32):
            return ctx.enter_context(nc.sbuf_tensor(name, shape, dt))

        def sem(name):
            return ctx.enter_context(nc.semaphore(name))

        x = sb("x", [P, TILES, D])
        xn = sb("xn", [P, TILES, D])
        xt = sb("xt", [P, KCH, TOKENS])
        yt = sb("yt", [P, KCH, TOKENS])
        wring = sb("wring", [P, 2, SLOT])
        gain = sb("gain", [P, D])
        toep = sb("toep", [P, HEADS, 2 * P])
        sbias = sb("sbias", [NS, HEADS, P + NS])
        ident2 = sb("ident2", [P, 2, P])
        sixteen = sb("sixteen", [P, TOP])
        relb = sb("relb", [N_BUCKETS + 1, HEADS])
        junk = sb("junk", [P, D])
        arena = sb("arena", [P, 16384])
        urow = arena[:, 0:BATCH * D].rearrange("p (k d) -> p k d", k=BATCH)
        vrow = arena[:, BATCH * D:2 * BATCH * D].rearrange("p (k d) -> p k d", k=BATCH)
        at = 0

        def take(n):
            nonlocal at
            at += n
            return arena[:, at - n:at]

        proj = take(TILES * IN_COLS).rearrange("p (i n) -> p i n", i=TILES)
        qt = take(NG * TOKENS).rearrange("p (g n) -> p g n", g=NG)
        kt = take(NG * TOKENS).rearrange("p (g n) -> p g n", g=NG)
        ckv = take(2 * 9 * P).rearrange("p (s c n) -> p s c n", s=2, c=9)
        lgp = take(2 * HEADS * 2 * P).rearrange("p (a h n) -> p a h n", a=2, h=HEADS)
        lgs = take(HEADS * (P + NS)).rearrange("p (h n) -> p h n", h=HEADS)
        scores = sb("scores", [P, 16 * NK])
        cand = sb("cand", [P, 16 * NK])
        qf = sb("qf", [P, 16, TOKENS])
        diag = sb("diag", [P, 2, BATCH, P])
        qff = qf[:, :, :].rearrange("p a n -> p (a n)")
        zt = qff[:, 0:3 * (SEQ + 2)].rearrange("p (c n) -> p c n", c=3)
        zs = qff[:, 800:800 + 3 * NB * 6].rearrange("p (c b t) -> p c b t", c=3, b=NB)
        gt = qff[:, 960:960 + 3 * TOKENS].rearrange("p (c n) -> p c n", c=3)
        acc = qff[:, 1840:1840 + 3 * TOKENS].rearrange("p (c n) -> p c n", c=3)
        ycm = qff[:, 2720:2720 + TILES * 384].rearrange("p (i n) -> p i n", i=TILES)
        pts = qff[:, 3880:3880 + HEADS * NS].rearrange("p (h n) -> p h n", h=HEADS)
        pte = qff[:, 4080:4080 + HEADS * NS].rearrange("p (h n) -> p h n", h=HEADS)
        lgt = qff[:, 4280:4280 + HEADS * NS].rearrange("p (h n) -> p h n", h=HEADS)
        pnew = qff[:, 4480:4480 + NG * NS].rearrange("p (g n) -> p g n", g=NG)
        pt0 = diag[:, 0, 0:6, :]
        pt1 = scores[:, 0:12 * P].rearrange("p (s n) -> p s n", s=12)
        qbs = [qff[:, 960:960 + NT * AW].rearrange("p (t n) -> p t n", t=NT), scores[:, 0:NT * AW].rearrange("p (t n) -> p t n", t=NT)]
        xnf = xn[:, :, :].rearrange("p i n -> p (i n)")
        cval = [ckv[:, 0], ckv[:, 1]] + [xnf[:, 9 * P * j:9 * P * (j + 1)].rearrange("p (c n) -> p c n", c=9) for j in range(2)]
        kq = cand[:, 0:NT * AW].rearrange("p (t n) -> p t n", t=NT)
        sqk = yt[:, :, :].rearrange("p a n -> p (a n)").rearrange("p (i n) -> p i n", i=TILES)
        sqv = xt[:, :, :].rearrange("p a n -> p (a n)")[:, 0:TILES * CW].rearrange("p (i n) -> p i n", i=TILES)
        wide = arena[:, 0:HEADS * PITCH].rearrange("p (h n) -> p h n", h=HEADS)
        gqk = sb("gqk", [P, 2, HD])
        gcv = sb("gcv", [P, CW])
        crow = sb("crow", [3, BW])
        brow = sb("brow", [CH, P])
        srow = sb("srow", [2 * NB, BW])
        cws = junk[:, 0:CH * P].rearrange("p (h n) -> p h n", h=CH)
        wmt = diag[:, 1, 0:CH, :]
        wss = sb("wss", [NS, CH, NS])
        bst = sb("bst", [P, CH])
        bss = sb("bss", [NS, CH])
        cwt = sb("cwt", [P, 3, 3])
        ssq = sb("ssq", [P, TILES])
        hss = sb("hss", [P, TILES, 2 * HEADS + CH])
        nmax = sb("nmax", [P, HEADS])
        nall = sb("nall", [P, 2])
        dmax = sb("dmax", [P, HEADS])
        qss = sb("qss", [NS, HEADS])
        esum = sb("esum", [P, HEADS])
        part = sb("part", [P, HEADS])
        total = sb("total", [P, 2])
        share = sb("share", [P, HEADS])
        kraw = sb("kraw", [P, 2, P])
        ktt = sb("ktt", [P, 2, P])
        top = sb("top", [P, 16, TOP])
        topi = sb("topi", [P, 16, TOP], U32)
        topf = junk[:, 0:256].rearrange("p (j k) -> p j k", j=16)
        ts = sb("ts", [P, PH, TOP])
        ti = sb("ti", [P, PH, TOP], U32)
        tab = junk[:, 256:512].bitcast(U32).rearrange("p (a k) -> p a k", a=2)
        tabf = junk[:, 512:768].rearrange("p (a k) -> p a k", a=2)
        pos = junk[:, 768:1024].rearrange("p (a k) -> p a k", a=2)
        eidx = sb("eidx", [P, PICKS])
        gmax = sb("gmax", [P, PH // 2])
        gsum = sb("gsum", [P, PH // 2])
        layer0 = sb("layer0", [P, 1])
        idx = sb("idx", [P, ALL_B * BATCH], U32)
        gate = sb("gate", [P, ALL_B * BATCH])
        idx2 = sb("idx2", [NS, PICKS], U32)
        gate2 = sb("gate2", [NS, PICKS])
        stage = sb("stage", [P, 2, BATCH], U32)
        hid = sb("hid", [P, 2, BATCH])
        act = sb("act", [P, 2, BATCH])
        cprompt = wring[0:N_BUCKETS + 1, 0, 0:NG * PITCH].rearrange("p (g n) -> p g n", g=NG)
        csample = wring[0:N_BUCKETS + 1, 1, 0:NG * NT * (P + NS)].rearrange("p (g t n) -> p g t n", g=NG, t=NT)
        cturn = wring[0:N_BUCKETS + 1, 0, 1200:1200 + NT * NS]
        cother = wring[0:NS, 1, 2000:2000 + P + NS]
        relw = cand[0:N_BUCKETS + 1, 0:HEADS * P].rearrange("p (h n) -> p h n", h=HEADS)
        relt = cand[0:N_BUCKETS + 1, 1024:1024 + HEADS * P].rearrange("p (h n) -> p h n", h=HEADS)

        bank = [ctx.enter_context(nc.psum_tensor(f"bank{i}", [P, 512], F32)) for i in range(8)]
        skew = nc.dram_tensor("skew", (HEADS, P, PITCH), F32, kind="Internal").ap()
        qrows = nc.dram_tensor("qrows", (NS, AW), F32, kind="Internal").ap()

        tick = {e: sem(f"tick_{e}") for e in ("pe", "act", "dve", "pool", "sp")}
        x_loaded, const_loaded, cleared, wss_clear = sem("x_loaded"), sem("const_loaded"), sem("cleared"), sem("wss_clear")
        rel_ready, bias_ps, bias_wide, bias_sample = sem("rel_ready"), sem("bias_ps"), sem("bias_wide"), sem("bias_sample")
        skew_written, toep_loaded = sem("skew_written"), sem("toep_loaded")
        gain_loaded, small_loaded, keys_loaded = sem("gain_loaded"), sem("small_loaded"), sem("keys_loaded")
        w_loaded = [sem("w_loaded0"), sem("w_loaded1")]
        square_sum, rms_mean, rms_root = sem("square_sum"), sem("rms_mean"), sem("rms_root")
        xn_done, xt_ps, xt_done = sem("xn_done"), sem("xt_ps"), sem("xt_done")
        prep_ps, prep_done, wmt_done, cblock_loaded = sem("prep_ps"), sem("prep_done"), sem("wmt_done"), sem("cblock_loaded")
        proj_ps, proj_done = sem("proj_ps"), sem("proj_done")
        squares, head_mean, head_root = sem("squares"), sem("head_mean"), sem("head_root")
        zb_done, qkv_done = sem("zb_done"), sem("qkv_done")
        zg_ps, zg_done, yb_done = sem("zg_ps"), sem("zg_done"), sem("yb_done")
        mix_ps, yc_done, yct_ps, yct_done = sem("mix_ps"), sem("yc_done"), sem("yct_ps"), sem("yct_done")
        qkt_ps, qkt_done = sem("qkt_ps"), sem("qkt_done")
        logit_ps, max_done, exp_done, prob_done = sem("logit_ps"), sem("max_done"), sem("exp_done"), sem("prob_done")
        probt_ps, probt_done, ya_ps, ya_done = sem("probt_ps"), sem("probt_done"), sem("ya_ps"), sem("ya_done")
        cache_in, kq_done, pv_done = [sem(f"cache_in{j}") for j in range(4)], sem("kq_done"), sem("pv_done")
        q_square, q_mean, q_root, q_ready, q_written = sem("q_square"), sem("q_mean"), sem("q_root"), sem("q_ready"), sem("q_written")
        kq_summed = sem("kq_summed")
        pnew_ps, pnew_done, yas_done = sem("pnew_ps"), sem("pnew_done"), sem("yas_done")
        rows_out, shift_out, y_out = sem("rows_out"), sem("shift_out"), sem("y_out")
        h_ps, h_done = sem("h_ps"), sem("h_done")
        keyt_ps, keyt_done, qf_ps, qf_done = sem("keyt_ps"), sem("keyt_done"), sem("qf_ps"), sem("qf_done")
        score_ps, score_done, pick_done, gexp_done, route_done = (
            sem("score_ps"), sem("score_done"), sem("pick_done"), sem("gexp_done"), sem("route_done"))
        xrep_loaded, idxrep_loaded = sem("xrep_loaded"), sem("idxrep_loaded")
        staged = sem("staged")
        u_in = [sem(f"u_in{k}") for k in range(BATCH)]
        v_in = [sem(f"v_in{k}") for k in range(BATCH)]
        dot_done, act_done, diag_done, v_used, y_ps, x_done = (
            sem("dot_done"), sem("act_done"), sem("diag_done"), sem("v_used"), sem("y_ps"), sem("x_done"))

        N_ROWS = 1 + 2 + 2 + NG * NT + 1 + 2 + 1

        def hold(eng, s, value, name):
            eng.wait_ge(s, value)
            eng.sem_inc(tick[name], 1)

        ident = ident2[:, 0, :]

        def score_bank(i, half):
            return 6 if i == 0 and half == 0 else 2 * half

        block = ctx.enter_context(nc.Block())

        @block.sync
        def _(sp):
            sp.sem_inc(proj_done, 6)
            sp.sem_inc(qf_done, 4)
            sp.sem_inc(h_done, 12)
            sp.sem_inc(kq_done, 2)
            sp.sem_inc(dot_done, BATCH)
            sp.sem_inc(v_used, 2 * BATCH)
            sp.dma_start(cprompt, io["c_prompt"]).then_inc(const_loaded, 16)
            sp.dma_start(csample, io["c_sample"].rearrange("p (g t n) -> p g t n", g=NG, t=NT)).then_inc(const_loaded, 16)
            sp.dma_start(cturn, io["c_turn"]).then_inc(const_loaded, 16)
            sp.dma_start(cother, io["c_other"]).then_inc(const_loaded, 16)
            sp.dma_start(ident2[:, :, :], io["c_ident"].rearrange("p (a n) -> p a n", a=2)).then_inc(const_loaded, 16)
            sp.dma_start(sixteen[:, :], io["c_sixteen"]).then_inc(const_loaded, 16)
            sp.dma_start(relb[0:N_BUCKETS, :], io["rel_bias"]).then_inc(const_loaded, 16)
            sp.dma_start(x[:, 0:2, :], io["x_prompt"][0].rearrange("(i p) d -> p i d", p=P)).then_inc(x_loaded, 16)
            sp.wait_ge(cleared, 1)
            sp.dma_start(x[0:NS, 2, :], io["x_sample"].rearrange("b t d -> (b t) d")).then_inc(x_loaded, 16)
            sp.wait_ge(bias_sample, 1)
            with sp.Fori(0, DEPTH) as l:
                hold(sp, h_done, 12 * l + 12, "sp")
                sp.dma_start(gain[:, :], io["norm_mix"][l].partition_broadcast(P)).then_inc(gain_loaded, 16)
                sp.dma_start(gqk[:, 0, :], io["q_norm"][l].partition_broadcast(P)).then_inc(small_loaded, 16)
                sp.dma_start(gqk[:, 1, :], io["k_norm"][l].partition_broadcast(P)).then_inc(small_loaded, 16)
                sp.dma_start(gcv[:, :], io["c_v_norm"].rearrange("l h d -> l (h d)")[l].partition_broadcast(P)).then_inc(small_loaded, 16)
                sp.dma_start(crow[:, :], io["conv_w"][l]).then_inc(small_loaded, 16)
                sp.dma_start(brow[:, :], io["c_bs"][l]).then_inc(small_loaded, 16)
                sp.dma_start(srow[:, :], io["state_b_conv"].rearrange("l b j n -> l (b j) n")[l]).then_inc(small_loaded, 16)
                hold(sp, x_done, 3 * l + 3, "sp")
                sp.dma_start(cws, io["c_ws"].rearrange("l h t s -> l t h s")[l]).then_inc(small_loaded, 16)
                sp.dma_start(kraw[:, 0, :], io["peer_k1"][l]).then_inc(keys_loaded, 16)
                sp.dma_start(kraw[:, 1, :], io["peer_k2"][l]).then_inc(keys_loaded, 16)
                w_in = io["w_in"].rearrange("l (k p) n -> l p k n", p=P)[l]
                w_out = io["w_out"].rearrange("l (k p) n -> l p k n", p=P)[l]
                w_q = io["peer_wq"].rearrange("l (k p) n -> l p k n", p=P)[l]
                def stream(n, width, src, copied, value, per_chunk):
                    with sp.Fori(0, n // 2) as c:
                        for s in range(2):
                            sp.wait_ge(copied, value + per_chunk * (2 * c + s))
                            sp.dma_start(wring[:, s, 0:KCH * width].rearrange("p (k n) -> p k n", k=KCH),
                                         src[:, :, bass.ds((2 * c + s) * width, width)]).then_inc(w_loaded[s], 16)

                hold(sp, qf_done, 16 * l + 4, "sp")
                stream(N_IN, W_IN, w_in, proj_done, 24 * l + 3, 3)
                hold(sp, xn_done, 6 * l + 3, "sp")
                sp.dma_start(gain[:, :], io["norm_ffn"][l].partition_broadcast(P)).then_inc(gain_loaded, 16)
                hold(sp, proj_done, 24 * l + 30, "sp")
                stream(N_OUT, W_OUT, w_out, h_done, 12 * l + 9, 3)
                hold(sp, h_done, 12 * l + 24, "sp")
                stream(N_Q, W_Q, w_q, qf_done, 16 * l + 2, 2)
                hold(sp, xn_done, 6 * l + 6, "sp")
                for q in range(1, 4):
                    sp.dma_start(xn[NS * q:NS * q + NS, 2, :], xn[0:NS, 2, :]).then_inc(xrep_loaded, 16)
                hold(sp, route_done, 6 * l + 6, "sp")
                for q in range(4):
                    dst = slice(NS * q, NS * q + NS), slice(COL0[2], COL0[2] + NS)
                    sp.dma_start(idx[dst[0], dst[1]], idx2[:, q * NS:q * NS + NS]).then_inc(idxrep_loaded, 16)
                    sp.dma_start(gate[dst[0], dst[1]], gate2[:, q * NS:q * NS + NS]).then_inc(idxrep_loaded, 16)
            sp.wait_ge(x_done, 3 * DEPTH + 3)
            sp.dma_start(io["y_prompt"][0].rearrange("(i p) d -> p i d", p=P), x[:, 0:2, :]).then_inc(y_out, 16)
            sp.dma_start(io["y_sample"].rearrange("b t d -> (b t) d"), x[0:NS, 2, :]).then_inc(y_out, 16)
            sp.wait_ge(y_out, 32)
            sp.wait_ge(shift_out, 16 * 3 * NB * DEPTH)
            sp.wait_ge(rows_out, 16 * N_ROWS * DEPTH)

        @block.gpsimd
        def _(pool):
            pool.memset(x[:, 2, :], 0.0).then_inc(cleared, 1)
            pool.wait_ge(bias_wide, 1)
            pool.dma_start(skew.rearrange("h p n -> p h n"), wide[:, :, :]).then_inc(skew_written, 16)
            pool.wait_ge(skew_written, 16)
            pool.dma_start(toep[:, :, :], bass.AP(tensor=skew.tensor, offset=P - 1,
                                                  ap=[[PITCH - 1, P], [P * PITCH, HEADS], [1, 2 * P]])).then_inc(toep_loaded, 16)
            pool.wait_ge(wss_clear, 1)
            c128, c512, c2048 = io["cache_a_kv_w128"], io["cache_a_kv_w512"], io["cache_a_kv_w2048"]
            near = c128.rearrange("l b m k h d -> l b m k (h d)")
            mid = c512.rearrange("l b (m t) k h d -> l b m t k (h d)", t=4)
            far = c2048.rearrange("l b (m t) k h d -> l b m t k (h d)", t=16)

            def load_cache(l, b, s, kv):
                pool.dma_start(cval[s][:, 0:4, :], mid[l, b, :, :, kv, :]).then_inc(cache_in[s], 16)
                pool.dma_start(cval[s][:, 4:8, :], far[l, b, :, 0:4, kv, :]).then_inc(cache_in[s], 16)
                pool.dma_start(cval[s][:, 8, :], near[l, b, :, kv, :]).then_inc(cache_in[s], 16)

            with pool.Fori(0, DEPTH) as l:
                hold(pool, x_done, 3 * l + 3, "pool")
                hold(pool, prep_done, l + 1, "pool")
                pool.affine_select(out=wmt[:, :, :], in_=wmt[:, :, :], pattern=[[0, CH], [1, P]], compare_op=ALU.is_ge,
                                   fill=0.0, base=0, channel_multiplier=-1).then_inc(wmt_done, 1)
                hold(pool, wmt_done, l + 1, "pool")
                for b in range(NB):
                    r = slice(b * NT, b * NT + NT)
                    pool.dma_start(wss[r, :, r], wmt[0:NT, :, 0:NT]).then_inc(cblock_loaded, 16)
                    pool.dma_start(bss[r, :], bst[0:NT, :]).then_inc(cblock_loaded, 16)
                hold(pool, q_ready, l + 1, "pool")
                pool.dma_start(qrows, proj[0:NS, 2, Q0:Q0 + AW]).then_inc(q_written, 16)
                hold(pool, q_written, 16 * (l + 1), "pool")
                with pool.Fori(0, NB // 2) as c:
                    for s in range(2):
                        hold(pool, kq_done, 8 * l + 2 * c + s + 1, "pool")
                        load_cache(l, 2 * c + s, s, 0)
                        pool.dma_start(qbs[s], qrows.rearrange("(b t) n -> b t n", t=NT)[bass.ds(2 * c + s, 1)].squeeze(0).partition_broadcast(P)).then_inc(cache_in[s], 16)
                for s in range(4):
                    if s < 2:
                        hold(pool, kq_done, 8 * l + 9 + s, "pool")
                    load_cache(l, s, s, 1)
                hold(pool, qkv_done, l + 1, "pool")
                kvn = proj[:, :, K0:K0 + 2 * AW].rearrange("p i (k n) -> p i k n", k=2)
                out_p = [io["kvp128"], io["kvp512"], io["kvp2048"]]
                out_s = [io["kvs128"], io["kvs512"], io["kvs2048"]]
                for g, (win, _) in enumerate(GROUPS):
                    cols = slice(g * P, g * P + P)
                    for i in range(2):
                        if min(win, SEQ) == SEQ or i == 1:
                            r0 = i * P if min(win, SEQ) == SEQ else 0
                            pool.dma_start(out_p[g].rearrange("l b r k h d -> l b r k (h d)")[l, 0, r0:r0 + P],
                                           kvn[:, i, :, cols]).then_inc(rows_out, 16)
                    for t in range(NT):
                        pool.dma_start(out_s[g].rearrange("l b r k h d -> l b r k (h d)")[l, :, win - NT + t],
                                       kvn[t:NS:NT, 2, :, cols]).then_inc(rows_out, 16)
                pool.dma_start(io["conv_prompt"][l, 0], proj[P - 2:P, 1, XB0:XB0 + BW]).then_inc(rows_out, 16)
                for j in range(2):
                    pool.dma_start(io["conv_sample"][l, :, j], proj[NT - 2 + j:NS:NT, 2, XB0:XB0 + BW]).then_inc(rows_out, 16)
                pool.dma_start(io["chunk_v"].rearrange("l b t h d -> l (b t) (h d)")[l],
                               proj[0:NS, 2, CV0:CV0 + CW]).then_inc(rows_out, 16)
                for s in range(4):
                    hold(pool, pv_done, 8 * l + s + 1, "pool")
                    load_cache(l, 4 + s, s, 1)
                hold(pool, rows_out, 16 * N_ROWS * (l + 1), "pool")
                for i, half in ((0, 0), (0, 1), (1, 0), (1, 1), (2, 0)):
                    if i < 2:
                        hold(pool, route_done, 6 * l + 2 * i + half + 1, "pool")
                        lo, hi = 4 * half, 4 * half + 4
                    else:
                        hold(pool, idxrep_loaded, 128 * (l + 1), "pool")
                        lo, hi = 0, 2
                    with pool.Fori(lo, hi) as c:
                        for s in range(2):
                            n = ALL_B * l + BASE[i] + 2 * c + s
                            hold(pool, v_used, BATCH * n + BATCH, "pool")
                            pool.tensor_copy(stage[:, s, :], idx[:, bass.ds(COL0[i] + (2 * c + s) * BATCH, BATCH)]).then_inc(staged, 1)
                            hold(pool, staged, n + 1, "pool")
                            for k in range(BATCH):
                                hold(pool, dot_done, BATCH * n + k + 1, "pool")
                                pool.indirect_dma_start(
                                    out=urow[:, k, :], out_offset=None, in_=io["peer_u"].rearrange("l e d -> (l e) d"),
                                    in_offset=bass.IndirectOffsetOnAxis(ap=stage[:, s, k:k + 1], axis=0)).then_inc(u_in[k], 16)
                            for k in range(BATCH):
                                hold(pool, v_used, BATCH * n + BATCH + k + 1, "pool")
                                pool.indirect_dma_start(
                                    out=vrow[:, k, :], out_offset=None, in_=io["peer_v"].rearrange("l e d -> (l e) d"),
                                    in_offset=bass.IndirectOffsetOnAxis(ap=stage[:, s, k:k + 1], axis=0)).then_inc(v_in[k], 16)

        @block.scalar
        def _(a):
            a.wait_ge(x_loaded, 32)
            a.sem_inc(x_done, 3)
            for h in range(HEADS):
                a.wait_ge(bias_ps, h + 1)
                last = a.activation(wide[:, h, :], bank[h][:, 0:PITCH], ACT.Copy)
            last.then_inc(bias_wide, 1)

            def norm(l, which):
                for i in range(TILES):
                    last = a.activation(xn[:, i, :], x[:, i, :], ACT.Square, accum_out=ssq[:, i:i + 1])
                last.then_inc(square_sum, 1)
                a.wait_ge(rms_mean, 2 * l + which + 1)
                a.activation(ssq[:, :], ssq[:, :], ACT.Sqrt).then_inc(rms_root, 1)
                for j in range(2 * TILES):
                    i, half = j // 2, j % 2
                    hold(a, xt_ps, 12 * l + 6 * which + j + 1, "act")
                    a.activation(xt[:, 4 * half:4 * half + 4, T0[i]:T0[i] + ROWS[i]],
                                 bank[j][:, :].rearrange("p (c n) -> p c n", c=4)[:, :, 0:ROWS[i]], ACT.Copy).then_inc(xt_done, 1)

            def exps(l, slot, n, rows, logits):
                a.wait_ge(max_done, 3 * l + slot + 1)
                a.activation(share[0:rows, :], dmax[0:rows, :], ACT.Exp)
                for h in range(HEADS):
                    last = a.activation(logits[0:rows, h, 0:n], logits[0:rows, h, 0:n], ACT.Exp,
                                        bias=nmax[0:rows, h:h + 1], accum_out=esum[0:rows, h:h + 1])
                last.then_inc(exp_done, 1)

            def batches(l, i, lo, hi):
                with a.Fori(lo // 2, hi // 2) as c:
                    for s in range(2):
                        n = ALL_B * l + BASE[i] + 2 * c + s
                        a.wait_ge(dot_done, BATCH * n + 2 * BATCH)
                        a.activation(act[:, s, :], hid[:, s, :], ACT.Gelu_apprx_tanh).then_inc(act_done, 1)

            def score_copy(l, i, half):
                a.wait_ge(score_ps, 6 * l + 2 * i + half + 1)
                r = ROWS[i]
                for j in range(2):
                    last = a.activation(scores[0:r, 1024 * half + 512 * j:1024 * half + 512 * j + 512],
                                        bank[score_bank(i, half) + j][0:r, :], ACT.Copy)
                last.then_inc(score_done, 1)

            def gate_exp(l, i, half):
                r, hs = ROWS[i], slice(4 * half, 4 * half + 4)
                hold(a, pick_done, 6 * l + 2 * i + half + 1, "act")
                a.activation(ts[0:r, hs, :], ts[0:r, hs, :], ACT.Exp).then_inc(gexp_done, 1)

            def y_copy(l, i):
                b0 = 4 + 2 * (i % 2)
                a.wait_ge(y_ps, 3 * l + i + 1)
                for half in range(2):
                    last = a.activation(x[:, i, 512 * half:512 * half + 512], bank[b0 + half][:, :], ACT.Copy)
                last.then_inc(x_done, 1)

            with a.Fori(0, DEPTH) as l:
                with a.Fori(0, NB) as b:
                    for (win, _), src, dst in zip(GROUPS, ("cache_a_kv_w128", "cache_a_kv_w512", "cache_a_kv_w2048"),
                                                  ("kvs128", "kvs512", "kvs2048")):
                        s_ = io[src].rearrange("l b r k h d -> l b (r k h d)")[l, b, NT * 256:win * 256]
                        d_ = io[dst].rearrange("l b r k h d -> l b (r k h d)")[l, b, 0:(win - NT) * 256]
                        a.dma_start(d_.rearrange("(q n) -> q n", q=16), s_.rearrange("(q n) -> q n", q=16)).then_inc(shift_out, 16)
                hold(a, x_done, 3 * l + 3, "act")
                norm(l, 0)
                hold(a, prep_ps, l + 1, "act")
                a.activation(wmt[:, 0:4, :], bank[6][:, :].rearrange("p (h n) -> p h n", h=4), ACT.Copy)
                a.activation(wmt[:, 4, :], bank[7][:, 0:P], ACT.Copy)
                a.activation(bst[:, :], bank[7][:, P:P + CH], ACT.Copy)
                a.activation(cwt[:, 0:2, :], bank[7][:, 136:142].rearrange("p (c j) -> p c j", c=2), ACT.Copy)
                a.activation(cwt[0:64, 2, :], bank[7][0:64, 142:145], ACT.Copy)
                a.activation(zs[:, 0:2, :, 0:2], bank[7][:, 160:192].rearrange("p (c b j) -> p c b j", c=2, b=NB), ACT.Copy)
                a.activation(zs[0:64, 2, :, 0:2], bank[7][0:64, 192:208].rearrange("p (b j) -> p b j", b=NB), ACT.Copy).then_inc(prep_done, 1)
                def proj_copy(lo, hi):
                    with a.Fori(lo, hi) as c:
                        for s in range(2):
                            for i in range(TILES):
                                hold(a, proj_ps, 24 * l + 6 * c + 3 * s + i + 1, "act")
                                a.activation(proj[0:ROWS[i], i, bass.ds((2 * c + s) * W_IN, W_IN)],
                                             bank[3 * s + i][0:ROWS[i], 0:W_IN], ACT.Copy).then_inc(proj_done, 1)
                    a.drain()

                a.wait_ge(skew_written, 16)
                proj_copy(0, 1)
                a.activation(sqk[0:NS, 2, 0:AW], proj[0:NS, 2, Q0:Q0 + AW], ACT.Square).then_inc(q_square, 1)
                hold(a, q_mean, l + 1, "act")
                a.activation(qss[:, :], qss[:, :], ACT.Sqrt).then_inc(q_root, 1)
                proj_copy(1, N_IN // 2)
                for i in range(TILES):
                    r = ROWS[i]
                    c0 = 0 if i < 2 else AW
                    last = a.activation(sqk[0:r, i, c0:], proj[0:r, i, c0:2 * AW], ACT.Square)
                last.then_inc(squares, 1)
                for i in range(TILES):
                    r = ROWS[i]
                    a.activation(proj[0:r, i, U0:U0 + 2 * CW], proj[0:r, i, U0:U0 + 2 * CW], ACT.Gelu_apprx_tanh)
                a.drain()
                for i in range(TILES):
                    r = ROWS[i]
                    last = a.activation(sqv[0:r, i, :], proj[0:r, i, CV0:CV0 + CW], ACT.Square)
                last.then_inc(squares, 1)
                for i in range(TILES):
                    r, t0, bz, bg = ROWS[i], T0[i], bank[2 * i], bank[2 * i + 1]
                    hold(a, zg_ps, 3 * l + i + 1, "act")
                    gv = bg[:, 0:384].rearrange("p (c n) -> p c n", c=3)
                    zv = bz[:, 0:384].rearrange("p (c n) -> p c n", c=3)
                    a.activation(gt[:, 0:2, t0:t0 + r], gv[:, 0:2, 0:r], ACT.Copy)
                    a.activation(gt[0:64, 2, t0:t0 + r], gv[0:64, 2, 0:r], ACT.Copy)
                    if i < 2:
                        a.activation(zt[:, 0:2, 2 + t0:2 + t0 + r], zv[:, 0:2, 0:r], ACT.Copy)
                        a.activation(zt[0:64, 2, 2 + t0:2 + t0 + r], zv[0:64, 2, 0:r], ACT.Copy).then_inc(zg_done, 1)
                    else:
                        for ch in range(3):
                            w = 128 if ch < 2 else 64
                            last = a.activation(zs[0:w, ch, :, 2:6], zv[0:w, ch, 0:r].rearrange("p (b t) -> p b t", b=NB), ACT.Copy)
                        last.then_inc(zg_done, 1)
                hold(a, head_mean, l + 1, "act")
                a.activation(hss[:, :, :], hss[:, :, :], ACT.Sqrt).then_inc(head_root, 1)
                for i in range(TILES):
                    r, t0 = ROWS[i], T0[i]
                    hold(a, yct_ps, 3 * l + i + 1, "act")
                    v = bank[2 * i][:, 0:384].rearrange("p (c n) -> p c n", c=3)
                    a.activation(yt[64:128, 5, t0:t0 + r], v[64:128, 0, 0:r], ACT.Copy)
                    a.activation(yt[:, 6:8, t0:t0 + r], v[:, 1:3, 0:r], ACT.Copy).then_inc(yct_done, 1)
                for j in range(2 * TILES):
                    i = j // 2
                    r, t0 = ROWS[i], T0[i]
                    hold(a, qkt_ps, 6 * l + j + 1, "act")
                    v = bank[1 + 2 * (j % 4)][:, 0:384].rearrange("p (c n) -> p c n", c=3)
                    a.activation((kt if j % 2 else qt)[:, :, t0:t0 + r], v[:, :, 0:r], ACT.Copy).then_inc(qkt_done, 1)
                for q in range(2):
                    exps(l, q, P * (q + 1), P, lgp[:, q])
                    hold(a, probt_ps, 3 * l + q + 1, "act")
                    if q == 0:
                        a.activation(pt0[:, 0:4, :], bank[0][:, :].rearrange("p (s n) -> p s n", s=4), ACT.Copy)
                        last = a.activation(pt0[:, 4:6, :], bank[2][:, 0:256].rearrange("p (s n) -> p s n", s=2), ACT.Copy)
                    else:
                        for j in range(3):
                            last = a.activation(pt1[:, 4 * j:4 * j + 4, :],
                                                bank[1 + 2 * j][:, :].rearrange("p (s n) -> p s n", s=4), ACT.Copy)
                    last.then_inc(probt_done, 1)
                    hold(a, ya_ps, 2 * l + q + 1, "act")
                    a.activation(yt[:, 0:3, q * P:q * P + P],
                                 bank[4 + 3 * q][:, 0:384].rearrange("p (g n) -> p g n", g=NG), ACT.Copy).then_inc(ya_done, 1)
                exps(l, 2, P + NS, NS, lgs)
                hold(a, probt_ps, 3 * l + 3, "act")
                a.activation(pts[:, :, :], bank[4][:, 0:HEADS * NS].rearrange("p (h n) -> p h n", h=HEADS), ACT.Copy)
                a.activation(pte[0:NS, :, :], bank[5][0:NS, 0:HEADS * NS].rearrange("p (h n) -> p h n", h=HEADS), ACT.Copy).then_inc(probt_done, 1)
                hold(a, pnew_ps, l + 1, "act")
                a.activation(pnew[:, :, :], bank[7][:, 0:NG * NS].rearrange("p (g n) -> p g n", g=NG), ACT.Copy).then_inc(pnew_done, 1)
                hold(a, h_done, 12 * l + 24, "act")
                norm(l, 1)
                hold(a, keyt_ps, l + 1, "act")
                a.activation(ktt[:, :, :], bank[6][:, 0:256].rearrange("p (j n) -> p j n", j=2), ACT.Copy).then_inc(keyt_done, 1)
                def qf_copy(lo, hi):
                    with a.Fori(lo, hi) as c:
                        for s in range(2):
                            for j in range(2):
                                hold(a, qf_ps, 16 * l + 4 * c + 2 * s + j + 1, "act")
                                a.activation(qf[:, bass.ds(4 * c + 2 * s + j, 1), :], bank[2 * s + j][:, 0:TOKENS].unsqueeze(1), ACT.Copy).then_inc(qf_done, 1)

                qf_copy(0, N_Q // 4)
                score_copy(l, 0, 0)
                qf_copy(N_Q // 4, N_Q // 2)
                gate_exp(l, 0, 0)
                score_copy(l, 0, 1)
                batches(l, 0, 0, 2)
                gate_exp(l, 0, 1)
                a.wait_ge(route_done, 6 * l + 2)
                score_copy(l, 1, 0)
                score_copy(l, 1, 1)
                batches(l, 0, 2, 6)
                gate_exp(l, 1, 0)
                batches(l, 0, 6, 10)
                gate_exp(l, 1, 1)
                a.wait_ge(route_done, 6 * l + 4)
                score_copy(l, 2, 0)
                score_copy(l, 2, 1)
                batches(l, 0, 10, 14)
                gate_exp(l, 2, 0)
                batches(l, 0, 14, 16)
                y_copy(l, 0)
                batches(l, 1, 0, 2)
                gate_exp(l, 2, 1)
                batches(l, 1, 2, 16)
                y_copy(l, 1)
                batches(l, 2, 0, 4)
                y_copy(l, 2)

        @block.vector
        def _(v):
            v.memset(relb[N_BUCKETS:N_BUCKETS + 1, :], 1.0)
            v.memset(wss[:, :, :], 0.0).then_inc(wss_clear, 1)
            v.memset(hss[:, :, :], 1.0)
            v.memset(layer0[:, :], 0.0)
            v.drain()
            v.wait_ge(const_loaded, 112)
            v.tensor_copy(relw, relb[:, :].unsqueeze(2).broadcast_to([N_BUCKETS + 1, HEADS, P]))
            v.tensor_tensor(relt, relb[:, :].unsqueeze(2).broadcast_to([N_BUCKETS + 1, HEADS, P]),
                            cturn.unsqueeze(1).broadcast_to([N_BUCKETS + 1, HEADS, P]), ALU.mult).then_inc(rel_ready, 1)
            v.wait_ge(bias_ps, HEADS + 1)
            for j in range(2):
                last = v.tensor_tensor(sbias[:, 3 * j:3 * j + 3, :],
                                       bank[6 + j][0:NS, 0:480].rearrange("p (h n) -> p h n", h=3),
                                       cother.unsqueeze(1).broadcast_to([NS, 3, P + NS]), ALU.add)
            last.then_inc(bias_sample, 1)

            def norm(l, which):
                v.wait_ge(square_sum, 2 * l + which + 1)
                v.tensor_scalar(ssq[:, :], ssq[:, :], 1.0 / D, EPS, ALU.mult, ALU.add).then_inc(rms_mean, 1)
                v.wait_ge(rms_root, 2 * l + which + 1)
                v.reciprocal(ssq[:, :], ssq[:, :])
                v.drain()
                hold(v, gain_loaded, 32 * l + 16 * which + 16, "dve")
                for i in range(TILES):
                    v.scalar_tensor_tensor(out=xn[:, i, :], in0=x[:, i, :], scalar=ssq[:, i:i + 1], in1=gain[:, :],
                                           op0=ALU.mult, op1=ALU.mult).then_inc(xn_done, 1)

            def softmax(l, slot, n, rows, logits):
                lg = logits[0:rows, :, 0:n]
                v.drain()
                v.tensor_reduce(nmax[0:rows, :], lg, AX.X, ALU.max, negate=True)
                v.drain()
                by_head = nmax[0:rows, :].rearrange("p (g h) -> p h g", h=2)
                v.tensor_reduce(nall[0:rows, :], by_head, AX.X, ALU.min)
                v.drain()
                v.tensor_tensor(dmax[0:rows, :].rearrange("p (g h) -> p g h", h=2),
                                nall[0:rows, :].unsqueeze(1).broadcast_to([rows, NG, 2]),
                                nmax[0:rows, :].rearrange("p (g h) -> p g h", h=2), ALU.subtract).then_inc(max_done, 1)
                v.wait_ge(exp_done, 3 * l + slot + 1)
                v.tensor_tensor(part[0:rows, :], esum[0:rows, :], share[0:rows, :], ALU.mult)
                v.drain()
                v.tensor_reduce(total[0:rows, :], part[0:rows, :].rearrange("p (g h) -> p h g", h=2), AX.X, ALU.add)
                v.drain()
                v.reciprocal(total[0:rows, :], total[0:rows, :])
                v.drain()
                v.tensor_tensor(part[0:rows, :].rearrange("p (g h) -> p g h", h=2),
                                share[0:rows, :].rearrange("p (g h) -> p g h", h=2),
                                total[0:rows, :].unsqueeze(1).broadcast_to([rows, NG, 2]), ALU.mult)
                v.drain()
                v.tensor_tensor(lg, lg, part[0:rows, :].unsqueeze(2).broadcast_to([rows, HEADS, n]), ALU.mult).then_inc(prob_done, 1)

            def route(l, i, half):
                r = ROWS[i]
                hh, jj = PH // 2, PH
                c0, c1 = 1024 * half, 1024 * half + 1024
                s3 = scores[0:r, c0:c1].rearrange("p (j n) -> p j n", j=jj)
                c3 = cand[0:r, c0:c1].rearrange("p (j n) -> p j n", j=jj)
                top_, topi_, topf_ = (b[0:r, jj * half:jj * half + jj, :] for b in (top, topi, topf))
                ts_, ti_ = (b[0:r, hh * half:hh * half + hh, :] for b in (ts, ti))
                ps = slice(hh * TOP * half, hh * TOP * (half + 1))
                picks = hh * TOP
                v.drain()
                hold(v, score_done, 6 * l + 2 * i + half + 1, "dve")
                for j in range(jj):
                    v.max(top_[:, j, 0:8], s3[:, j, :])
                v.drain()
                for j in range(jj):
                    v.max_index(topi_[:, j, 0:8], top_[:, j, 0:8], s3[:, j, :])
                    v.match_replace(c3[:, j, :], top_[:, j, 0:8], s3[:, j, :], LOW)
                v.drain()
                for j in range(jj):
                    v.max(top_[:, j, 8:16], c3[:, j, :])
                v.drain()
                for j in range(jj):
                    v.max_index(topi_[:, j, 8:16], top_[:, j, 8:16], c3[:, j, :])
                v.drain()
                v.tensor_copy(topf_, topi_)
                t4 = top_.rearrange("p (h s) k -> p h s k", s=2)
                pair = cand[0:r, c0:c1].rearrange("p (h a b) -> p h a b", h=hh, a=TOP)
                for h in range(hh):
                    v.tensor_tensor(pair[:, h], t4[:, h, 0, :].unsqueeze(2).broadcast_to([r, TOP, TOP]),
                                    t4[:, h, 1, :].unsqueeze(1).broadcast_to([r, TOP, TOP]), ALU.add)
                v.drain()
                p3 = cand[0:r, c0:c1].rearrange("p (h n) -> p h n", h=hh)
                q3 = scores[0:r, c0:c1].rearrange("p (h n) -> p h n", h=hh)
                for h in range(hh):
                    v.max(ts_[:, h, 0:8], p3[:, h, :])
                v.drain()
                for h in range(hh):
                    v.max_index(ti_[:, h, 0:8], ts_[:, h, 0:8], p3[:, h, :])
                    v.match_replace(q3[:, h, :], ts_[:, h, 0:8], p3[:, h, :], LOW)
                v.drain()
                for h in range(hh):
                    v.max(ts_[:, h, 8:16], q3[:, h, :])
                v.drain()
                for h in range(hh):
                    v.max_index(ti_[:, h, 8:16], ts_[:, h, 8:16], q3[:, h, :])
                v.tensor_copy(gmax[0:r, :], ts_[:, :, 0])
                v.drain()
                v.tensor_tensor(ts_, ts_, gmax[0:r, :].unsqueeze(2).broadcast_to([r, hh, TOP]), ALU.subtract).then_inc(pick_done, 1)
                tif = ti_.rearrange("p h k -> p (h k)")
                v.tensor_scalar(tab[0:r, 0, ps], tif, 4, None, ALU.logical_shift_right)
                v.tensor_scalar(tab[0:r, 1, ps], tif, 15, None, ALU.bitwise_and)
                v.drain()
                v.tensor_copy(tabf[0:r, :, ps], tab[0:r, :, ps])
                v.drain()
                f4 = topf_.rearrange("p (h s) k -> p h s k", s=2)
                for key, buf in ((0, scores), (1, cand)):
                    hot = buf[0:r, c0:c1].rearrange("p (n a) -> p n a", a=TOP)
                    v.tensor_tensor(hot, sixteen[0:r, :].unsqueeze(1).broadcast_to([r, picks, TOP]),
                                    tabf[0:r, key, ps].unsqueeze(2).broadcast_to([r, picks, TOP]), ALU.is_equal)
                v.drain()
                for key, buf in ((0, scores), (1, cand)):
                    hot = buf[0:r, c0:c1].rearrange("p (h k a) -> p h k a", h=hh, k=TOP)
                    for h in range(hh):
                        v.tensor_tensor(hot[:, h], hot[:, h], f4[:, h, key, :].unsqueeze(1).broadcast_to([r, TOP, TOP]), ALU.mult)
                v.drain()
                for key, buf in ((0, scores), (1, cand)):
                    v.tensor_reduce(pos[0:r, key, ps], buf[0:r, c0:c1].rearrange("p (n a) -> p n a", a=TOP), AX.X, ALU.add)
                v.drain()
                v.scalar_tensor_tensor(out=eidx[0:r, ps], in0=pos[0:r, 0, ps], scalar=float(NK), in1=pos[0:r, 1, ps],
                                       op0=ALU.mult, op1=ALU.add)
                v.drain()
                cols = slice(COL0[i] + ps.start, COL0[i] + ps.stop) if i < 2 else ps
                to_i, to_g = (idx[:, cols], gate[:, cols]) if i < 2 else (idx2[:, cols], gate2[:, cols])
                v.tensor_scalar(to_i, eidx[0:r, ps], layer0[0:r, :], None, ALU.add)
                hold(v, gexp_done, 6 * l + 2 * i + half + 1, "dve")
                v.tensor_reduce(gsum[0:r, :], ts_, AX.X, ALU.add)
                v.drain()
                v.reciprocal(gsum[0:r, :], gsum[0:r, :])
                v.drain()
                v.tensor_tensor(to_g.rearrange("p (h k) -> p h k", h=hh), ts_,
                                gsum[0:r, :].unsqueeze(2).broadcast_to([r, hh, TOP]), ALU.mult).then_inc(route_done, 1)

            def batches(l, i, lo, hi):
                mask = ident2[:, 0 if i < 2 else 1, :]
                with v.Fori(lo // 2, hi // 2) as c:
                    for s in range(2):
                        n = ALL_B * l + BASE[i] + 2 * c + s
                        for k in range(BATCH):
                            v.wait_ge(u_in[k], 16 * n + 16)
                            v.scalar_tensor_tensor(out=urow[:, k, :], in0=urow[:, k, :], scalar=1.0, in1=xn[:, i, :],
                                                   op0=ALU.mult, op1=ALU.mult, accum_out=hid[:, s, k:k + 1]).then_inc(dot_done, 1)
                        hold(v, v_used, BATCH * n + BATCH, "dve")
                        hold(v, act_done, n + 1, "dve")
                        for k in range(BATCH):
                            last = v.tensor_scalar(diag[:, s, k, :], mask, act[:, s, k:k + 1],
                                                   gate[:, bass.ds(COL0[i] + (2 * c + s) * BATCH + k, 1)], ALU.mult, ALU.mult)
                        last.then_inc(diag_done, 1)

            with v.Fori(0, DEPTH) as l:
                norm(l, 0)
                hold(v, q_square, l + 1, "dve")
                v.tensor_reduce(qss[:, :], sqk[0:NS, 2, 0:AW].rearrange("p (h d) -> p h d", d=HD), AX.X, ALU.add)
                v.drain()
                v.tensor_scalar(qss[:, :], qss[:, :], 1.0 / HD, EPS, ALU.mult, ALU.add).then_inc(q_mean, 1)
                hold(v, q_root, l + 1, "dve")
                v.reciprocal(qss[:, :], qss[:, :])
                v.drain()
                qs = proj[0:NS, 2, Q0:Q0 + AW].rearrange("p (h d) -> p h d", d=HD)
                v.tensor_tensor(qs, qs, qss[:, :].unsqueeze(2).broadcast_to([NS, HEADS, HD]), ALU.mult)
                v.drain()
                hold(v, small_loaded, 112 * (l + 1), "dve")
                v.tensor_tensor(qs, qs, gqk[0:NS, 0, :].unsqueeze(1).broadcast_to([NS, HEADS, HD]), ALU.mult).then_inc(q_ready, 1)
                with v.Fori(0, NB // 2) as c:
                    for s in range(2):
                        b = 2 * c + s
                        hold(v, cache_in[s], 352 * l + 64 * (c + 1), "dve")
                        for t in range(NT):
                            v.tensor_tensor(kq[:, t, P:3 * P].rearrange("p (g n) -> p g n", g=2), qbs[s][:, t, P:3 * P].rearrange("p (g n) -> p g n", g=2),
                                            ckv[:, s, t:8:4, :], ALU.mult)
                            last = v.tensor_tensor(kq[:, t, 0:P], qbs[s][:, t, 0:P], ckv[:, s, 8, :], ALU.mult)
                        last.then_inc(kq_done, 1)
                        v.drain()
                        v.tensor_reduce(lgt[:, :, bass.ds(b * NT, NT)].rearrange("p h t -> p t h"),
                                        kq[:, :, :].rearrange("p t (h d) -> p t h d", d=HD), AX.X, ALU.add)
                        v.drain()
                v.drain().then_inc(kq_summed, 1)
                hold(v, squares, 2 * l + 1, "dve")
                for i in range(TILES):
                    r = ROWS[i]
                    last = v.tensor_tensor(proj[0:r, i, XB0:XB0 + BW], proj[0:r, i, GC0:GC0 + BW], proj[0:r, i, XB0:XB0 + BW], ALU.mult)
                last.then_inc(zb_done, 1)
                for i in range(TILES):
                    r = ROWS[i]
                    h0 = 0 if i < 2 else HEADS
                    v.tensor_reduce(hss[0:r, i, h0:2 * HEADS], sqk[0:r, i, h0 * HD:].rearrange("p (h d) -> p h d", d=HD), AX.X, ALU.add)
                hold(v, squares, 2 * l + 2, "dve")
                for i in range(TILES):
                    r = ROWS[i]
                    v.tensor_reduce(hss[0:r, i, 2 * HEADS:], sqv[0:r, i, :].rearrange("p (h d) -> p h d", d=HD), AX.X, ALU.add)
                v.drain()
                v.tensor_scalar(hss[:, :, :], hss[:, :, :], 1.0 / HD, EPS, ALU.mult, ALU.add).then_inc(head_mean, 1)
                hold(v, head_root, l + 1, "dve")
                v.reciprocal(hss[:, :, :], hss[:, :, :])
                v.drain()
                for i in range(TILES):
                    r = ROWS[i]
                    h0 = 0 if i < 2 else HEADS
                    qk = proj[0:r, i, h0 * HD:2 * AW].rearrange("p (h d) -> p h d", d=HD)
                    vc = proj[0:r, i, CV0:CV0 + CW].rearrange("p (h d) -> p h d", d=HD)
                    v.tensor_tensor(vc, vc, hss[0:r, i, 2 * HEADS:].unsqueeze(2).broadcast_to([r, CH, HD]), ALU.mult)
                    v.tensor_tensor(qk, qk, hss[0:r, i, h0:2 * HEADS].unsqueeze(2).broadcast_to([r, 2 * HEADS - h0, HD]), ALU.mult)
                v.drain()
                for i in range(TILES):
                    r = ROWS[i]
                    vc = proj[0:r, i, CV0:CV0 + CW]
                    v.tensor_tensor(vc, vc, gcv[0:r, :], ALU.mult)
                    for j in range(0 if i < 2 else 1, 2):
                        qk = proj[0:r, i, j * AW:(j + 1) * AW].rearrange("p (h d) -> p h d", d=HD)
                        last = v.tensor_tensor(qk, qk, gqk[0:r, j, :].unsqueeze(1).broadcast_to([r, HEADS, HD]), ALU.mult)
                last.then_inc(qkv_done, 1)
                v.memset(zt[:, :, 0:2], 0.0)
                for i in range(TILES):
                    v.memset(ycm[:, i, 0:64], 0.0)
                v.drain()
                hold(v, zg_done, 3 * l + 3, "dve")
                for j in range(3):
                    for ch in range(3):
                        w = 128 if ch < 2 else 64
                        tap = cwt[0:w, ch, j:j + 1]
                        for src, dst in ((zt[0:w, ch, j:j + SEQ], acc[0:w, ch, 0:SEQ]),
                                         (zs[0:w, ch, :, j:j + NT], acc[0:w, ch, SEQ:TOKENS].rearrange("p (b t) -> p b t", b=NB))):
                            if j == 0:
                                v.tensor_scalar(dst, src, tap, None, ALU.mult)
                            else:
                                v.scalar_tensor_tensor(out=dst, in0=src, scalar=tap, in1=dst, op0=ALU.mult, op1=ALU.add)
                    v.drain()
                v.tensor_tensor(yt[:, 3:5, :], acc[:, 0:2, :], gt[:, 0:2, :], ALU.mult)
                v.tensor_tensor(yt[0:64, 5, :], acc[0:64, 2, :], gt[0:64, 2, :], ALU.mult).then_inc(yb_done, 1)
                hold(v, cblock_loaded, 256 * (l + 1), "dve")
                for i in range(TILES):
                    r = ROWS[i]
                    bs = (bst if i < 2 else bss)[0:r, :]
                    hold(v, mix_ps, 3 * l + i + 1, "dve")
                    mixed = ycm[0:r, i, 64:64 + CW]
                    v.tensor_tensor(mixed.rearrange("p (h d) -> p h d", d=HD),
                                    bank[6 + i % 2][0:r, 0:CW].rearrange("p (h d) -> p h d", d=HD),
                                    bs.unsqueeze(2).broadcast_to([r, CH, HD]), ALU.add)
                    v.drain()
                    v.tensor_tensor(mixed, mixed, proj[0:r, i, U0:U0 + CW], ALU.mult).then_inc(yc_done, 1)
                v.wait_ge(toep_loaded, 16)
                for q in range(2):
                    n = P * (q + 1)
                    hold(v, logit_ps, 3 * l + q + 1, "dve")
                    for m, heads in enumerate(((0, 2), (1, 3), (4,), (5,))):
                        k = len(heads)
                        hs = slice(heads[0], heads[-1] + 1, 2)
                        v.scalar_tensor_tensor(out=lgp[:, q, hs, 0:n], in0=bank[2 * m + q][:, 0:k * 256].rearrange("p (h n) -> p h n", h=k)[:, :, 0:n],
                                               scalar=SCALE, in1=toep[:, hs, 2 * P - n:2 * P], op0=ALU.mult, op1=ALU.add)
                    softmax(l, q, n, P, lgp[:, q])
                hold(v, logit_ps, 3 * l + 3, "dve")
                for j in range(2):
                    k = 4 - 2 * j
                    v.scalar_tensor_tensor(out=lgs[0:NS, 4 * j:4 * j + k, 0:P], in0=bank[j][0:NS, 0:k * P].rearrange("p (h n) -> p h n", h=k),
                                           scalar=SCALE, in1=sbias[:, 4 * j:4 * j + k, 0:P], op0=ALU.mult, op1=ALU.add)
                    v.scalar_tensor_tensor(out=lgs[0:NS, j:HEADS:2, P:P + NS], in0=bank[2 + j][0:NS, 0:NG * NS].rearrange("p (h n) -> p h n", h=NG),
                                           scalar=SCALE, in1=sbias[:, j:HEADS:2, P:P + NS], op0=ALU.mult, op1=ALU.add)
                softmax(l, 2, P + NS, NS, lgs)
                hold(v, pnew_done, l + 1, "dve")
                hold(v, pv_done, 8 * l + 8, "dve")
                pvc = bank[6][:, 0:NG * NS * 2].rearrange("p (g n h) -> p g n h", g=NG, h=2)
                for h in range(2):
                    r = slice(64 * h, 64 * h + 64)
                    last = v.tensor_tensor(yt[r, 0:3, SEQ:TOKENS], pvc[r, :, :, h], pnew[r, :, :], ALU.add)
                last.then_inc(yas_done, 1)
                with v.Fori(0, N_OUT // 2) as c:
                    for s in range(2):
                        for i in range(TILES):
                            r = ROWS[i]
                            v.wait_ge(h_ps, 12 * l + 6 * c + 3 * s + i + 1)
                            xs = x[0:r, i, bass.ds((2 * c + s) * W_OUT, W_OUT)]
                            v.tensor_tensor(xs, bank[3 * s + i][0:r, 0:W_OUT], xs, ALU.add).then_inc(h_done, 1)
                norm(l, 1)
                route(l, 0, 0)
                batches(l, 0, 0, 2)
                route(l, 0, 1)
                batches(l, 0, 2, 6)
                route(l, 1, 0)
                batches(l, 0, 6, 10)
                route(l, 1, 1)
                batches(l, 0, 10, 14)
                route(l, 2, 0)
                batches(l, 0, 14, 16)
                batches(l, 1, 0, 2)
                route(l, 2, 1)
                batches(l, 1, 2, 16)
                hold(v, xrep_loaded, 48 * (l + 1), "dve")
                hold(v, idxrep_loaded, 128 * (l + 1), "dve")
                batches(l, 2, 0, 4)
                v.tensor_scalar(layer0[:, :], layer0[:, :], float(NE), None, ALU.add)

        @block.tensor
        def _(pe):
            pe.wait_ge(rel_ready, 1)
            for h in range(HEADS):
                pe.matmul(bank[h][:, 0:PITCH], relw[:, h, :], cprompt[:, h // 2, :], start=True, stop=True).then_inc(bias_ps, 1)
            for h in range(HEADS):
                o = bank[6 + h // 3][0:NS, (h % 3) * 160:(h % 3) * 160 + 160]
                for t in range(NT):
                    last = pe.matmul(o, relt[:, h, t * NS:t * NS + NS], csample[:, h // 2, t, :], start=(t == 0), stop=(t == NT - 1))
            last.then_inc(bias_ps, 1)
            pe.wait_ge(bias_sample, 1)
            pe.wait_ge(bias_wide, 1)

            def norm_t(l, which):
                for j in range(2 * TILES):
                    i, half = j // 2, j % 2
                    r = ROWS[i]
                    if half == 0:
                        hold(pe, xn_done, 6 * l + 3 * which + i + 1, "pe")
                    for c in range(4):
                        last = pe.transpose(bank[j][:, c * P:c * P + r], xn[0:r, i, (4 * half + c) * P:(4 * half + c + 1) * P], ident[0:r, 0:r])
                    last.then_inc(xt_ps, 1)
                hold(pe, xt_done, 12 * l + 6 * which + 6, "pe")

            def score(l, i, half):
                r, b0 = ROWS[i], score_bank(i, half)
                for j in range(8):
                    last = pe.matmul(bank[b0 + j // 4][0:r, (j % 4) * P:(j % 4 + 1) * P], qf[:, 8 * half + j, T0[i]:T0[i] + r], ktt[:, j % 2, :],
                                     start=True, stop=True)
                last.then_inc(score_ps, 1)

            def open_y(l, i):
                b0 = 4 + 2 * (i % 2)
                if i == 2:
                    hold(pe, x_done, 3 * l + 4, "pe")
                for half in range(2):
                    pe.matmul(bank[b0 + half][:, :], ident[0:64, :], x[0:64, i, 512 * half:512 * half + 512], start=True, stop=False)

            def batches(l, i, lo, hi):
                b0 = 4 + 2 * (i % 2)
                with pe.Fori(lo // 2, hi // 2) as c:
                    for s in range(2):
                        n = ALL_B * l + BASE[i] + 2 * c + s
                        hold(pe, diag_done, n + 1, "pe")
                        for k in range(BATCH):
                            hold(pe, v_in[k], 16 * n + 16, "pe")
                            for half in range(2):
                                last = pe.matmul(bank[b0 + half][:, :], diag[:, s, k, :], vrow[:, k, 512 * half:512 * half + 512], start=False, stop=False)
                            last.then_inc(v_used, 1)

            def close_y(l, i):
                b0 = 4 + 2 * (i % 2)
                for half in range(2):
                    last = pe.matmul(bank[b0 + half][:, :], ident[64:128, :], x[64:128, i, 512 * half:512 * half + 512], start=False, stop=True)
                last.then_inc(y_ps, 1)

            with pe.Fori(0, DEPTH) as l:
                norm_t(l, 0)
                hold(pe, small_loaded, 112 * (l + 1), "pe")
                for h in range(CH):
                    pe.transpose(bank[6 + h // 4][:, (h % 4) * P:(h % 4 + 1) * P], cws[:, h, :], ident)
                pe.transpose(bank[7][:, P:P + CH], brow[:, :], ident[0:CH, 0:CH])
                for ch in range(3):
                    w = 128 if ch < 2 else 64
                    pe.transpose(bank[7][0:w, 136 + 3 * ch:139 + 3 * ch], crow[:, ch * P:ch * P + w], ident[0:3, 0:3])
                    last = pe.transpose(bank[7][0:w, 160 + 16 * ch:176 + 16 * ch], srow[:, ch * P:ch * P + w], ident[0:2 * NB, 0:2 * NB])
                last.then_inc(prep_ps, 1)
                with pe.Fori(0, N_IN // 2) as c:
                    for s in range(2):
                        w = wring[:, s, 0:KCH * W_IN].rearrange("p (k n) -> p k n", k=KCH)
                        hold(pe, w_loaded[s], 16 * (N_W // 2 * l + c + 1), "pe")
                        for i in range(TILES):
                            hold(pe, proj_done, 24 * l + 6 * c + 3 * s + i + 1, "pe")
                            for k in range(KCH):
                                last = pe.matmul(bank[3 * s + i][0:ROWS[i], 0:W_IN], xt[:, k, T0[i]:T0[i] + ROWS[i]], w[:, k, :],
                                                 start=(k == 0), stop=(k == KCH - 1))
                            last.then_inc(proj_ps, 1)
                hold(pe, zb_done, l + 1, "pe")
                for i in range(TILES):
                    r = ROWS[i]
                    for ch in range(3):
                        w = 128 if ch < 2 else 64
                        pe.transpose(bank[2 * i][0:w, ch * P:ch * P + r], proj[0:r, i, XB0 + ch * P:XB0 + ch * P + w], ident[0:r, 0:r])
                        last = pe.transpose(bank[2 * i + 1][0:w, ch * P:ch * P + r], proj[0:r, i, GB0 + ch * P:GB0 + ch * P + w], ident[0:r, 0:r])
                    last.then_inc(zg_ps, 1)
                hold(pe, qkv_done, l + 1, "pe")
                hold(pe, wmt_done, l + 1, "pe")
                for i in range(TILES):
                    r = ROWS[i]
                    if i == 2:
                        hold(pe, cblock_loaded, 256 * (l + 1), "pe")
                        hold(pe, yc_done, 3 * l + 1, "pe")
                    wt = wmt if i < 2 else wss
                    for h in range(CH):
                        last = pe.matmul(bank[6 + i % 2][0:r, h * HD:h * HD + HD], wt[0:r, h, 0:r],
                                         proj[0:r, i, CV0 + h * HD:CV0 + h * HD + HD], start=True, stop=True)
                    last.then_inc(mix_ps, 1)
                for i in range(TILES):
                    r = ROWS[i]
                    hold(pe, zg_done, 3 * l + i + 1, "pe")
                    hold(pe, yc_done, 3 * l + i + 1, "pe")
                    for ch in range(3):
                        last = pe.transpose(bank[2 * i][:, ch * P:ch * P + r], ycm[0:r, i, ch * P:ch * P + P], ident[0:r, 0:r])
                    last.then_inc(yct_ps, 1)
                for j in range(2 * TILES):
                    i = j // 2
                    r = ROWS[i]
                    if j >= 4:
                        hold(pe, qkt_done, 6 * l + j - 3, "pe")
                    for g in range(NG):
                        c0 = (K0 if j % 2 else Q0) + g * P
                        last = pe.transpose(bank[1 + 2 * (j % 4)][:, g * P:g * P + r], proj[0:r, i, c0:c0 + P], ident[0:r, 0:r])
                    last.then_inc(qkt_ps, 1)
                hold(pe, qkt_done, 6 * l + 6, "pe")
                hold(pe, yct_done, 3 * l + 3, "pe")

                def logits(q):
                    n = P * (q + 1)
                    for m, heads in enumerate(((0, 2), (1, 3), (4,), (5,))):
                        for j, h in enumerate(heads):
                            r = slice(64 * (h % 2), 64 * (h % 2) + 64)
                            last = pe.matmul(bank[2 * m + q][:, 256 * j:256 * j + n], qt[r, h // 2, q * P:q * P + P], kt[r, h // 2, 0:n],
                                             start=True, stop=True)
                    last.then_inc(logit_ps, 1)

                logits(0)
                logits(1)
                for q in range(2):
                    hold(pe, prob_done, 3 * l + q + 1, "pe")
                    for h in range(HEADS):
                        for kb in range(q + 1):
                            j = h * (q + 1) + kb
                            last = pe.transpose(bank[2 * (j // 4) + q][:, (j % 4) * P:(j % 4 + 1) * P], lgp[:, q, h, kb * P:kb * P + P], ident)
                    last.then_inc(probt_ps, 1)
                    hold(pe, probt_done, 3 * l + q + 1, "pe")
                    for h in range(HEADS):
                        r = slice(64 * (h % 2), 64 * (h % 2) + 64)
                        for kb in range(q + 1):
                            j = h * (q + 1) + kb
                            last = pe.matmul(bank[4 + 3 * q][r, (h // 2) * P:(h // 2 + 1) * P], proj[:, kb, V0 + h * HD:V0 + h * HD + HD],
                                             (pt0 if q == 0 else pt1)[:, j, :], start=(kb == 0), stop=(kb == q))
                    last.then_inc(ya_ps, 1)
                hold(pe, ya_done, 2 * l + 2, "pe")
                hold(pe, kq_summed, l + 1, "pe")
                for h in range(HEADS):
                    pe.transpose(bank[h // 4][0:NS, (h % 4) * P:(h % 4 + 1) * P], lgt[:, h, :], ident)
                for h in range(HEADS):
                    r = slice(64 * (h % 2), 64 * (h % 2) + 64)
                    last = pe.matmul(bank[2 + h % 2][0:NS, (h // 2) * NS:(h // 2 + 1) * NS], qt[r, h // 2, SEQ:TOKENS], kt[r, h // 2, SEQ:TOKENS],
                                     start=True, stop=True)
                last.then_inc(logit_ps, 1)
                hold(pe, prob_done, 3 * l + 3, "pe")
                for h in range(HEADS):
                    pe.transpose(bank[4][:, h * NS:h * NS + NS], lgs[0:NS, h, 0:P], ident[0:NS, 0:NS])
                    last = pe.transpose(bank[5][0:NS, h * NS:h * NS + NS], lgs[0:NS, h, P:P + NS], ident[0:NS, 0:NS])
                last.then_inc(probt_ps, 1)
                hold(pe, probt_done, 3 * l + 3, "pe")
                for h in range(HEADS):
                    r = slice(64 * (h % 2), 64 * (h % 2) + 64)
                    last = pe.matmul(bank[7][r, (h // 2) * NS:(h // 2 + 1) * NS], proj[0:NS, 2, V0 + h * HD:V0 + h * HD + HD], pte[0:NS, h, :],
                                     start=True, stop=True)
                last.then_inc(pnew_ps, 1)
                pvc = bank[6][:, 0:NG * NS * 2].rearrange("p (g n h) -> p g n h", g=NG, h=2)
                with pe.Fori(0, NB // 4) as c:
                    for s in range(4):
                        hold(pe, cache_in[s], (352 * l + 256 if s < 2 else 96 * l) + 48 * (c + 1), "pe")
                        for t in range(NT):
                            for g in range(NG):
                                slot = 8 if g == 0 else 4 * (g - 1) + t
                                n = (4 * c + s) * NT + t
                                last = pe.matmul(pvc[:, g, bass.ds(n, 1), :].rearrange("p n h -> p (n h)"), cval[s][:, slot, :],
                                                 pts[:, 2 * g:2 * g + 2, bass.ds(n, 1)].rearrange("p h n -> p (h n)"), start=True, stop=True)
                        last.then_inc(pv_done, 1)
                hold(pe, yas_done, l + 1, "pe")
                hold(pe, yb_done, l + 1, "pe")
                with pe.Fori(0, N_OUT // 2) as c:
                    for s in range(2):
                        w = wring[:, s, 0:KCH * W_OUT].rearrange("p (k n) -> p k n", k=KCH)
                        hold(pe, w_loaded[s], 16 * (N_W // 2 * l + N_IN // 2 + c + 1), "pe")
                        for i in range(TILES):
                            hold(pe, h_done, 12 * l + 6 * c + 3 * s + i + 7, "pe")
                            for k in range(KCH):
                                last = pe.matmul(bank[3 * s + i][0:ROWS[i], 0:W_OUT], yt[:, k, T0[i]:T0[i] + ROWS[i]], w[:, k, :],
                                                 start=(k == 0), stop=(k == KCH - 1))
                            last.then_inc(h_ps, 1)
                norm_t(l, 1)
                hold(pe, keys_loaded, 32 * (l + 1), "pe")
                for j in range(2):
                    last = pe.transpose(bank[6][:, j * P:j * P + P], kraw[:, j, :], ident)
                last.then_inc(keyt_ps, 1)
                def queries(lo, hi):
                    with pe.Fori(lo, hi) as c:
                        for s in range(2):
                            w = wring[:, s, 0:KCH * W_Q].rearrange("p (k n) -> p k n", k=KCH)
                            hold(pe, w_loaded[s], 16 * (N_W // 2 * l + (N_IN + N_OUT) // 2 + c + 1), "pe")
                            for j in range(2):
                                hold(pe, qf_done, 16 * l + 4 * c + 2 * s + j + 1, "pe")
                                for k in range(KCH):
                                    last = pe.matmul(bank[2 * s + j][:, 0:TOKENS], w[:, k, j * P:j * P + P], xt[:, k, :],
                                                     start=(k == 0), stop=(k == KCH - 1))
                                last.then_inc(qf_ps, 1)

                queries(0, N_Q // 4)
                hold(pe, keyt_done, l + 1, "pe")
                hold(pe, qf_done, 16 * l + 12, "pe")
                score(l, 0, 0)
                queries(N_Q // 4, N_Q // 2)
                hold(pe, qf_done, 16 * l + 20, "pe")
                score(l, 0, 1)
                hold(pe, score_done, 6 * l + 2, "pe")
                score(l, 1, 0)
                score(l, 1, 1)
                open_y(l, 0)
                batches(l, 0, 0, 6)
                hold(pe, score_done, 6 * l + 4, "pe")
                score(l, 2, 0)
                score(l, 2, 1)
                batches(l, 0, 6, 16)
                close_y(l, 0)
                open_y(l, 1)
                batches(l, 1, 0, 16)
                close_y(l, 1)
                open_y(l, 2)
                batches(l, 2, 0, 4)
                close_y(l, 2)


_INS = ("x_prompt", "x_sample", "cache_a_kv_w128", "cache_a_kv_w512", "cache_a_kv_w2048", "state_b_conv", "rel_bias",
        "norm_mix", "w_in", "q_norm", "k_norm", "conv_w", "c_v_norm", "c_ws", "c_bs", "w_out", "norm_ffn", "peer_wq",
        "peer_k1", "peer_k2", "peer_u", "peer_v")
_OUTS = (("y_prompt", (1, SEQ, D)), ("y_sample", (NB, NT, D)),
         ("kvp128", (DEPTH, 1, 128, 2, 2, HD)), ("kvs128", (DEPTH, NB, 128, 2, 2, HD)),
         ("kvp512", (DEPTH, 1, SEQ, 2, 2, HD)), ("kvs512", (DEPTH, NB, 512, 2, 2, HD)),
         ("kvp2048", (DEPTH, 1, SEQ, 2, 2, HD)), ("kvs2048", (DEPTH, NB, 2048, 2, 2, HD)),
         ("conv_prompt", (DEPTH, 1, 2, BW)), ("conv_sample", (DEPTH, NB, 2, BW)),
         ("chunk_v", (DEPTH, NB, NT, CH, HD)))


def kernel(**inputs):
    import concourse.bacc as bacc
    from concourse.bass_utils import run_bass_kernel_spmd as run

    nc = bacc.Bacc("TRN2", target_bir_lowering=False, num_devices=1)
    arrays = {name: np.ascontiguousarray(inputs[name]) for name in _INS}
    arrays.update(shape_constants())
    io = {name: nc.dram_tensor(name, a.shape, F32, kind="ExternalInput").ap() for name, a in arrays.items()}
    for name, shape in _OUTS:
        io[name] = nc.dram_tensor(name, shape, F32, kind="ExternalOutput").ap()
    trunk(nc, io)
    got = run(nc, [arrays], core_ids=[0]).results[0]
    return tuple(got[name] for name, _ in _OUTS)
```

```python
from contextlib import ExitStack

import numpy as np

import concourse.bass as bass
from concourse import mybir

F32 = mybir.dt.float32
U32 = mybir.dt.uint32
ACT = mybir.ActivationFunctionType
ALU = mybir.AluOpType
AX = mybir.AxisListType

P = 128
D = 1024
DEPTH = 2
SEQ = 256
NB, NT = 8, 4
NS = NB * NT
TOKENS = SEQ + NS
TILES = 3
ROWS = (P, P, NS)
T0 = (0, P, 2 * P)
HD = 64
GROUPS = ((128, 1), (512, 4), (2048, 16))
NG = len(GROUPS)
HEADS = 2 * NG
AW = HEADS * HD
BW = (D - AW) // 2
CW = D - AW - BW
CH = CW // HD
IN_COLS = 3 * AW + 3 * BW + 2 * CW
Q0, K0, V0 = 0, AW, 2 * AW
XB0, GB0, GC0 = 3 * AW, 3 * AW + BW, 3 * AW + 2 * BW
U0 = 3 * AW + 3 * BW
CV0 = U0 + CW
KCH = D // P
N_IN, W_IN = 8, IN_COLS // 8
N_OUT, W_OUT = 4, 256
N_Q, W_Q = 8, 256
N_W = N_IN + N_OUT + N_Q
SLOT = KCH * W_IN
N_BUCKETS = 32
REL_MAX = 2048
NEG = -1e30
EPS = 1e-6
SCALE = HD ** -0.5
PH = 8
NK = 128
NE = NK * NK
TOP = 16
PICKS = PH * TOP
BATCH = 8
BATCHES = (PICKS // BATCH, PICKS // BATCH, PICKS // BATCH // 4)
BASE = (0, BATCHES[0], 2 * BATCHES[0])
ALL_B = sum(BATCHES)
COL0 = (0, PICKS, 2 * PICKS)
PARTS = ((0, 0, 2), (0, 2, 4), (0, 4, 8), (1, 0, 4), (1, 4, 8), (2, 0, 4), (2, 4, 8))
NP = len(PARTS)
PITCH = 384
LOW = -3.0e38


def bucket(dist):
    d = np.maximum(np.asarray(dist), 0)
    half = N_BUCKETS // 2
    ratio = np.log(np.maximum(d, 1).astype(np.float32) / half) / np.log(REL_MAX / half)
    large = np.minimum(half + (ratio * (N_BUCKETS - half)).astype(np.int32), N_BUCKETS - 1)
    return np.where(d < half, d, large).astype(np.int32)


def shape_constants():
    prompt = np.zeros((N_BUCKETS + 1, NG, PITCH), np.float32)
    for g, (win, dil) in enumerate(GROUPS):
        for u in range(PITCH - 1):
            d = 255 - u
            if 0 <= d <= win and d % dil == 0:
                prompt[bucket(d), g, u] = 1
            else:
                prompt[N_BUCKETS, g, u] = NEG
    sample = np.zeros((N_BUCKETS + 1, NG, NT, P + NS), np.float32)
    for g, (win, dil) in enumerate(GROUPS):
        for t in range(NT):
            for m in range(P):
                d = P + t - m if g == 0 else win - dil * m
                if d <= win:
                    sample[bucket(d), g, t, m] = 1
                else:
                    sample[N_BUCKETS, g, t, m] = NEG
            for n in range(NS):
                d = t - n % NT
                if d == 0 or (g == 0 and d > 0):
                    sample[bucket(d), g, t, P + n] = 1
                else:
                    sample[N_BUCKETS, g, t, P + n] = NEG
    turn = np.zeros((N_BUCKETS + 1, NT, NS), np.float32)
    for t in range(NT):
        turn[:, t, t::NT] = 1
    other = np.zeros((NS, P + NS), np.float32)
    for n in range(NS):
        for k in range(NS):
            if n // NT != k // NT:
                other[n, P + k] = NEG
    ident = np.zeros((P, 2, P), np.float32)
    ident[:, 0] = np.eye(P)
    for p in range(P):
        ident[p, 1, p % NS] = 1
    sixteen = np.tile(np.arange(TOP, dtype=np.float32), (P, 1))
    return {
        "c_prompt": prompt, "c_sample": sample.reshape(N_BUCKETS + 1, -1), "c_turn": turn.reshape(N_BUCKETS + 1, -1),
        "c_other": other, "c_ident": ident.reshape(P, -1), "c_sixteen": sixteen,
    }


def trunk(nc, io):
    ctx = ExitStack()
    with ctx:
        def sb(name, shape, dt=F32):
            return ctx.enter_context(nc.sbuf_tensor(name, shape, dt))

        def sem(name):
            return ctx.enter_context(nc.semaphore(name))

        x = sb("x", [P, TILES, D])
        xn = sb("xn", [P, TILES, D])
        xt = sb("xt", [P, KCH, TOKENS])
        yt = sb("yt", [P, KCH, TOKENS])
        wring = sb("wring", [P, 2, SLOT])
        gain = sb("gain", [P, D])
        toep = sb("toep", [P, HEADS, 2 * P])
        sbias = sb("sbias", [NS, HEADS, P + NS])
        ident2 = sb("ident2", [P, 2, P])
        sixteen = sb("sixteen", [P, TOP])
        relb = sb("relb", [N_BUCKETS + 1, HEADS])
        junk = sb("junk", [P, D])
        arena = sb("arena", [P, 16384])
        urow = arena[:, 0:BATCH * D].rearrange("p (k d) -> p k d", k=BATCH)
        vrow = arena[:, BATCH * D:2 * BATCH * D].rearrange("p (k d) -> p k d", k=BATCH)
        at = 0

        def take(n):
            nonlocal at
            at += n
            return arena[:, at - n:at]

        proj = take(TILES * IN_COLS).rearrange("p (i n) -> p i n", i=TILES)
        qt = take(NG * TOKENS).rearrange("p (g n) -> p g n", g=NG)
        kt = take(NG * TOKENS).rearrange("p (g n) -> p g n", g=NG)
        ckv = take(2 * 9 * P).rearrange("p (s c n) -> p s c n", s=2, c=9)
        lgp = take(2 * HEADS * 2 * P).rearrange("p (a h n) -> p a h n", a=2, h=HEADS)
        lgs = take(HEADS * (P + NS)).rearrange("p (h n) -> p h n", h=HEADS)
        scores = sb("scores", [P, 16 * NK])
        cand = sb("cand", [P, 16 * NK])
        qf = sb("qf", [P, 16, TOKENS])
        diag = sb("diag", [P, 2, BATCH, P])
        qff = qf[:, :, :].rearrange("p a n -> p (a n)")
        zt = qff[:, 0:3 * (SEQ + 2)].rearrange("p (c n) -> p c n", c=3)
        zs = qff[:, 800:800 + 3 * NB * 6].rearrange("p (c b t) -> p c b t", c=3, b=NB)
        gt = qff[:, 960:960 + 3 * TOKENS].rearrange("p (c n) -> p c n", c=3)
        acc = qff[:, 1840:1840 + 3 * TOKENS].rearrange("p (c n) -> p c n", c=3)
        ycm = qff[:, 2720:2720 + TILES * 384].rearrange("p (i n) -> p i n", i=TILES)
        pts = qff[:, 3880:3880 + HEADS * NS].rearrange("p (h n) -> p h n", h=HEADS)
        pte = qff[:, 4080:4080 + HEADS * NS].rearrange("p (h n) -> p h n", h=HEADS)
        lgt = qff[:, 4280:4280 + HEADS * NS].rearrange("p (h n) -> p h n", h=HEADS)
        pnew = qff[:, 4480:4480 + NG * NS].rearrange("p (g n) -> p g n", g=NG)
        pt0 = diag[:, 0, 0:6, :]
        pt1 = scores[:, 0:12 * P].rearrange("p (s n) -> p s n", s=12)
        qbs = [qff[:, 960:960 + NT * AW].rearrange("p (t n) -> p t n", t=NT), scores[:, 0:NT * AW].rearrange("p (t n) -> p t n", t=NT)]
        xnf = xn[:, :, :].rearrange("p i n -> p (i n)")
        four = lambda ap: ap.rearrange("p (c n) -> p c n", c=4)
        whole = lambda ap: (four(ap[:, 0:4 * P]), four(ap[:, 4 * P:8 * P]), ap[:, 8 * P:9 * P])
        candf, xtf = cand[:, :], xt[:, :, :].rearrange("p a n -> p (a n)")
        cval = [(ckv[:, j, 0:4, :], ckv[:, j, 4:8, :], ckv[:, j, 8, :]) for j in range(2)]
        cval += [whole(xnf[:, 9 * P * j:9 * P * (j + 1)]) for j in range(2)]
        cval += [whole(candf[:, 0:9 * P]), (four(xnf[:, 19 * P:23 * P]), four(candf[:, 9 * P:13 * P]), candf[:, 13 * P:14 * P])]
        cval += [whole(xtf[:, 9 * P:18 * P]), (four(wring[:, 0, 16 * P:20 * P]), four(wring[:, 1, 16 * P:20 * P]), xnf[:, 18 * P:19 * P])]
        kq = cand[:, 0:NT * AW].rearrange("p (t n) -> p t n", t=NT)
        sqk = yt[:, :, :].rearrange("p a n -> p (a n)").rearrange("p (i n) -> p i n", i=TILES)
        sqv = xt[:, :, :].rearrange("p a n -> p (a n)")[:, 0:TILES * CW].rearrange("p (i n) -> p i n", i=TILES)
        wide = arena[:, 0:HEADS * PITCH].rearrange("p (h n) -> p h n", h=HEADS)
        gqk = sb("gqk", [P, 2, HD])
        gcv = sb("gcv", [P, CW])
        crow = sb("crow", [3, BW])
        brow = sb("brow", [CH, P])
        srow = sb("srow", [2 * NB, BW])
        cws = junk[:, 0:CH * P].rearrange("p (h n) -> p h n", h=CH)
        wmt = diag[:, 1, 0:CH, :]
        wss = sb("wss", [NS, CH, NS])
        bst = sb("bst", [P, CH])
        bss = sb("bss", [NS, CH])
        cwt = sb("cwt", [P, 3, 3])
        ssq = sb("ssq", [P, TILES])
        hss = sb("hss", [P, TILES, 2 * HEADS + CH])
        nmax = sb("nmax", [P, HEADS])
        nall = sb("nall", [P, 2])
        dmax = sb("dmax", [P, HEADS])
        qss = sb("qss", [NS, HEADS])
        esum = sb("esum", [P, HEADS])
        part = sb("part", [P, HEADS])
        total = sb("total", [P, 2])
        share = sb("share", [P, HEADS])
        kraw = sb("kraw", [P, 2, P])
        ktt = sb("ktt", [P, 2, P])
        top = sb("top", [P, 16, TOP])
        topi = sb("topi", [P, 16, TOP], U32)
        topf = junk[:, 0:256].rearrange("p (j k) -> p j k", j=16)
        ts = sb("ts", [P, PH, TOP])
        ti = sb("ti", [P, PH, TOP], U32)
        tab = junk[:, 256:512].bitcast(U32).rearrange("p (a k) -> p a k", a=2)
        tabf = junk[:, 512:768].rearrange("p (a k) -> p a k", a=2)
        pos = junk[:, 768:1024].rearrange("p (a k) -> p a k", a=2)
        eidx = sb("eidx", [P, PICKS])
        gmax = sb("gmax", [P, PH // 2])
        gsum = sb("gsum", [P, PH // 2])
        layer0 = sb("layer0", [P, 1])
        idx = sb("idx", [P, ALL_B * BATCH], U32)
        gate = sb("gate", [P, ALL_B * BATCH])
        idx2 = sb("idx2", [NS, PICKS], U32)
        gate2 = sb("gate2", [NS, PICKS])
        stage = sb("stage", [P, 2, BATCH], U32)
        hid = sb("hid", [P, 2, BATCH])
        act = sb("act", [P, 2, BATCH])
        cprompt = qff[0:N_BUCKETS + 1, 0:NG * PITCH].rearrange("p (g n) -> p g n", g=NG)
        csample = qff[0:N_BUCKETS + 1, 1200:1200 + NG * NT * (P + NS)].rearrange("p (g t n) -> p g t n", g=NG, t=NT)
        cturn = qff[0:N_BUCKETS + 1, 3200:3200 + NT * NS]
        cother = qff[0:NS, 3400:3400 + P + NS]
        relw = cand[0:N_BUCKETS + 1, 0:HEADS * P].rearrange("p (h n) -> p h n", h=HEADS)
        relt = cand[0:N_BUCKETS + 1, 1024:1024 + HEADS * P].rearrange("p (h n) -> p h n", h=HEADS)

        bank = [ctx.enter_context(nc.psum_tensor(f"bank{i}", [P, 512], F32)) for i in range(8)]
        old_ps = [bank[b][0:NS, 0:3 * P].rearrange("p (h n) -> p h n", h=3) for b in (4, 6)]
        new_ps = [bank[b][0:NS, 0:NG * NS].rearrange("p (h n) -> p h n", h=NG) for b in (0, 2)]
        pts_ps = bank[4][:, 0:HEADS * NS].rearrange("p (h n) -> p h n", h=HEADS)
        pte_ps = bank[4][:, 256:256 + HEADS * NS].rearrange("p (h n) -> p h n", h=HEADS)
        pnew_sum = bank[4][:, 0:NG * NS].rearrange("p (g n) -> p g n", g=NG)
        pv_sum = bank[6][:, 0:NG * NS * 2].rearrange("p (g h n) -> p g h n", g=NG, h=2)
        lg_ps = {0: (((0, 2, 4), bank[0]), ((1, 3, 5), bank[2])),
                 1: (((0, 2), bank[1]), ((1, 3), bank[3]), ((4,), bank[5]), ((5,), bank[7]))}
        prob_banks = {0: (bank[0], bank[2]), 1: (bank[1], bank[3], bank[5])}
        ya_bank = {0: bank[4], 1: bank[7]}
        skew = nc.dram_tensor("skew", (HEADS, P, PITCH), F32, kind="Internal").ap()
        qrows = nc.dram_tensor("qrows", (NS, AW), F32, kind="Internal").ap()

        tick = {e: sem(f"tick_{e}") for e in ("pe", "act", "dve", "pool", "sp")}
        x_loaded, const_loaded, cleared, wss_clear = sem("x_loaded"), sem("const_loaded"), sem("cleared"), sem("wss_clear")
        rel_ready, bias_ps, bias_wide, bias_sample = sem("rel_ready"), sem("bias_ps"), sem("bias_wide"), sem("bias_sample")
        skew_written, toep_loaded = sem("skew_written"), sem("toep_loaded")
        gain_loaded, small_loaded, keys_loaded = sem("gain_loaded"), sem("small_loaded"), sem("keys_loaded")
        w_loaded = [sem("w_loaded0"), sem("w_loaded1")]
        square_sum, rms_mean, rms_root = sem("square_sum"), sem("rms_mean"), sem("rms_root")
        xn_done, xt_ps, xt_done = sem("xn_done"), sem("xt_ps"), sem("xt_done")
        prep_ps, prep_done, wmt_done, cblock_loaded = sem("prep_ps"), sem("prep_done"), sem("wmt_done"), sem("cblock_loaded")
        proj_ps, proj_done = sem("proj_ps"), sem("proj_done")
        squares, head_mean, head_root = sem("squares"), sem("head_mean"), sem("head_root")
        zb_done, qkv_done = sem("zb_done"), sem("qkv_done")
        zg_ps, zg_done, yb_done = sem("zg_ps"), sem("zg_done"), sem("yb_done")
        mix_ps, yc_done, yct_ps, yct_done = sem("mix_ps"), sem("yc_done"), sem("yct_ps"), sem("yct_done")
        qkt_ps, qkt_done = sem("qkt_ps"), sem("qkt_done")
        logit_ps, max_done, exp_done, prob_done = sem("logit_ps"), sem("max_done"), sem("exp_done"), sem("prob_done")
        probt_ps, probt_done, ya_ps, ya_done = sem("probt_ps"), sem("probt_done"), sem("ya_ps"), sem("ya_done")
        cache_in, kq_done, pv_done = [sem(f"cache_in{j}") for j in range(NB)], sem("kq_done"), sem("pv_done")
        q_square, q_mean, q_root, q_ready, q_written = sem("q_square"), sem("q_mean"), sem("q_root"), sem("q_ready"), sem("q_written")
        kq_summed = sem("kq_summed")
        pnew_ps, pnew_done, yas_done = sem("pnew_ps"), sem("pnew_done"), sem("yas_done")
        rows_out, shift_out, y_out = sem("rows_out"), sem("shift_out"), sem("y_out")
        h_ps, h_done = sem("h_ps"), sem("h_done")
        keyt_ps, keyt_done, qf_ps, qf_done = sem("keyt_ps"), sem("keyt_done"), sem("qf_ps"), sem("qf_done")
        score_ps, score_done, pick_done, gexp_done, route_done = (
            sem("score_ps"), sem("score_done"), sem("pick_done"), sem("gexp_done"), sem("route_done"))
        xrep_loaded, idxrep_loaded = sem("xrep_loaded"), sem("idxrep_loaded")
        staged = sem("staged")
        u_in = [sem(f"u_in{k}") for k in range(BATCH)]
        v_in = [sem(f"v_in{k}") for k in range(BATCH)]
        dot_done, act_done, diag_done, v_used, y_ps, x_done = (
            sem("dot_done"), sem("act_done"), sem("diag_done"), sem("v_used"), sem("y_ps"), sem("x_done"))

        N_ROWS = 1 + 2 + 2 + NG * NT + 1 + 2 + 1

        def hold(eng, s, value, name):
            eng.wait_ge(s, value)
            eng.sem_inc(tick[name], 1)

        ident = ident2[:, 0, :]

        def score_bank(p):
            return (6, 7, 2, 0, 2, 0, 2)[p]

        block = ctx.enter_context(nc.Block())

        @block.sync
        def _(sp):
            sp.sem_inc(proj_done, 6)
            sp.sem_inc(qf_done, 4)
            sp.sem_inc(h_done, 12)
            sp.sem_inc(kq_done, 2)
            sp.sem_inc(dot_done, BATCH)
            sp.sem_inc(v_used, 2 * BATCH)
            sp.dma_start(relb[0:N_BUCKETS, :], io["rel_bias"]).then_inc(const_loaded, 16)
            sp.dma_start(cprompt, io["c_prompt"]).then_inc(const_loaded, 16)
            sp.dma_start(cturn, io["c_turn"]).then_inc(const_loaded, 16)
            sp.dma_start(csample, io["c_sample"].rearrange("p (g t n) -> p g t n", g=NG, t=NT)).then_inc(const_loaded, 16)
            sp.dma_start(cother, io["c_other"]).then_inc(const_loaded, 16)
            sp.dma_start(ident2[:, :, :], io["c_ident"].rearrange("p (a n) -> p a n", a=2)).then_inc(const_loaded, 16)
            sp.dma_start(sixteen[:, :], io["c_sixteen"]).then_inc(const_loaded, 16)
            sp.dma_start(x[:, 0:2, :], io["x_prompt"][0].rearrange("(i p) d -> p i d", p=P)).then_inc(x_loaded, 16)
            sp.wait_ge(cleared, 1)
            sp.dma_start(x[0:NS, 2, :], io["x_sample"].rearrange("b t d -> (b t) d")).then_inc(x_loaded, 16)
            with sp.Fori(0, DEPTH) as l:
                hold(sp, h_done, 12 * l + 12, "sp")
                sp.dma_start(gain[:, :], io["norm_mix"][l].partition_broadcast(P)).then_inc(gain_loaded, 16)
                sp.dma_start(gqk[:, 0, :], io["q_norm"][l].partition_broadcast(P)).then_inc(small_loaded, 16)
                sp.dma_start(gqk[:, 1, :], io["k_norm"][l].partition_broadcast(P)).then_inc(small_loaded, 16)
                sp.dma_start(gcv[:, :], io["c_v_norm"].rearrange("l h d -> l (h d)")[l].partition_broadcast(P)).then_inc(small_loaded, 16)
                sp.dma_start(crow[:, :], io["conv_w"][l]).then_inc(small_loaded, 16)
                sp.dma_start(brow[:, :], io["c_bs"][l]).then_inc(small_loaded, 16)
                sp.dma_start(srow[:, :], io["state_b_conv"].rearrange("l b j n -> l (b j) n")[l]).then_inc(small_loaded, 16)
                w_in = io["w_in"].rearrange("l (k p) n -> l p k n", p=P)[l]
                w_out = io["w_out"].rearrange("l (k p) n -> l p k n", p=P)[l]
                w_q = io["peer_wq"].rearrange("l (k p) n -> l p k n", p=P)[l]

                def stream(lo, hi, width, src, copied, value, per_chunk):
                    with sp.Fori(lo, hi) as c:
                        for s in range(2):
                            sp.wait_ge(copied, value + per_chunk * (2 * c + s))
                            sp.dma_start(wring[:, s, 0:KCH * width].rearrange("p (k n) -> p k n", k=KCH),
                                         src[:, :, bass.ds((2 * c + s) * width, width)]).then_inc(w_loaded[s], 16)

                hold(sp, qf_done, 16 * l + 4, "sp")
                stream(0, 1, W_IN, w_in, proj_done, 24 * l + 3, 3)
                hold(sp, x_done, 3 * l + 3, "sp")
                sp.dma_start(cws, io["c_ws"].rearrange("l h t s -> l t h s")[l]).then_inc(small_loaded, 16)
                sp.dma_start(kraw[:, 0, :], io["peer_k1"][l]).then_inc(keys_loaded, 16)
                sp.dma_start(kraw[:, 1, :], io["peer_k2"][l]).then_inc(keys_loaded, 16)
                stream(1, N_IN // 2, W_IN, w_in, proj_done, 24 * l + 3, 3)
                hold(sp, xn_done, 6 * l + 3, "sp")
                sp.dma_start(gain[:, :], io["norm_ffn"][l].partition_broadcast(P)).then_inc(gain_loaded, 16)
                hold(sp, proj_done, 24 * l + 30, "sp")
                stream(0, 1, W_OUT, w_out, h_done, 12 * l + 9, 3)
                hold(sp, qkv_done, l + 1, "sp")
                with sp.Fori(0, NB) as b:
                    for (win, _), src, dst in zip(GROUPS, ("cache_a_kv_w128", "cache_a_kv_w512", "cache_a_kv_w2048"),
                                                  ("kvs128", "kvs512", "kvs2048")):
                        s_ = io[src].rearrange("l b r k h d -> l b (r k h d)")[l, b, NT * 256:win * 256]
                        d_ = io[dst].rearrange("l b r k h d -> l b (r k h d)")[l, b, 0:(win - NT) * 256]
                        sp.dma_start(d_.rearrange("(q n) -> q n", q=16), s_.rearrange("(q n) -> q n", q=16)).then_inc(shift_out, 16)
                stream(1, N_OUT // 2, W_OUT, w_out, h_done, 12 * l + 9, 3)
                hold(sp, h_done, 12 * l + 24, "sp")
                stream(0, N_Q // 2, W_Q, w_q, qf_done, 16 * l + 2, 2)
                hold(sp, xn_done, 6 * l + 6, "sp")
                for q in range(1, 4):
                    sp.dma_start(xn[NS * q:NS * q + NS, 2, :], xn[0:NS, 2, :]).then_inc(xrep_loaded, 16)
                hold(sp, route_done, NP * (l + 1), "sp")
                for q in range(4):
                    dst = slice(NS * q, NS * q + NS), slice(COL0[2], COL0[2] + NS)
                    sp.dma_start(idx[dst[0], dst[1]], idx2[:, q * NS:q * NS + NS]).then_inc(idxrep_loaded, 16)
                    sp.dma_start(gate[dst[0], dst[1]], gate2[:, q * NS:q * NS + NS]).then_inc(idxrep_loaded, 16)
            sp.wait_ge(x_done, 3 * DEPTH + 3)
            sp.dma_start(io["y_prompt"][0].rearrange("(i p) d -> p i d", p=P), x[:, 0:2, :]).then_inc(y_out, 16)
            sp.dma_start(io["y_sample"].rearrange("b t d -> (b t) d"), x[0:NS, 2, :]).then_inc(y_out, 16)
            sp.wait_ge(y_out, 32)
            sp.wait_ge(shift_out, 16 * 3 * NB * DEPTH)
            sp.wait_ge(rows_out, 16 * N_ROWS * DEPTH)

        @block.gpsimd
        def _(pool):
            pool.memset(x[:, 2, :], 0.0).then_inc(cleared, 1)
            pool.wait_ge(bias_wide, 1)
            pool.dma_start(skew.rearrange("h p n -> p h n"), wide[:, :, :]).then_inc(skew_written, 16)
            pool.wait_ge(skew_written, 16)
            pool.dma_start(toep[:, :, :], bass.AP(tensor=skew.tensor, offset=P - 1,
                                                  ap=[[PITCH - 1, P], [P * PITCH, HEADS], [1, 2 * P]])).then_inc(toep_loaded, 16)
            pool.wait_ge(wss_clear, 1)
            c128, c512, c2048 = io["cache_a_kv_w128"], io["cache_a_kv_w512"], io["cache_a_kv_w2048"]
            near = c128.rearrange("l b m k h d -> l b m k (h d)")
            mid = c512.rearrange("l b (m t) k h d -> l b m t k (h d)", t=4)
            far = c2048.rearrange("l b (m t) k h d -> l b m t k (h d)", t=16)

            def load_cache(l, b, s, kv):
                pool.dma_start(cval[s][0], mid[l, b, :, :, kv, :]).then_inc(cache_in[s], 16)
                pool.dma_start(cval[s][1], far[l, b, :, 0:4, kv, :]).then_inc(cache_in[s], 16)
                pool.dma_start(cval[s][2], near[l, b, :, kv, :]).then_inc(cache_in[s], 16)

            with pool.Fori(0, DEPTH) as l:
                hold(pool, x_done, 3 * l + 3, "pool")
                hold(pool, prep_done, l + 1, "pool")
                pool.affine_select(out=wmt[:, :, :], in_=wmt[:, :, :], pattern=[[0, CH], [1, P]], compare_op=ALU.is_ge,
                                   fill=0.0, base=0, channel_multiplier=-1).then_inc(wmt_done, 1)
                hold(pool, wmt_done, l + 1, "pool")
                for b in range(NB):
                    r = slice(b * NT, b * NT + NT)
                    pool.dma_start(wss[r, :, r], wmt[0:NT, :, 0:NT]).then_inc(cblock_loaded, 16)
                    pool.dma_start(bss[r, :], bst[0:NT, :]).then_inc(cblock_loaded, 16)
                hold(pool, q_ready, l + 1, "pool")
                pool.dma_start(qrows, proj[0:NS, 2, Q0:Q0 + AW]).then_inc(q_written, 16)
                hold(pool, q_written, 16 * (l + 1), "pool")
                with pool.Fori(0, NB // 2) as c:
                    for s in range(2):
                        hold(pool, kq_done, 8 * l + 2 * c + s + 1, "pool")
                        load_cache(l, 2 * c + s, s, 0)
                        pool.dma_start(qbs[s], qrows.rearrange("(b t) n -> b t n", t=NT)[bass.ds(2 * c + s, 1)].squeeze(0).partition_broadcast(P)).then_inc(cache_in[s], 16)
                for s in (2, 3, 0, 1, 4, 5, 6, 7):
                    if s < 2:
                        hold(pool, kq_done, 8 * l + 9 + s, "pool")
                    if s == 4:
                        hold(pool, kq_summed, l + 1, "pool")
                    if s == 6:
                        hold(pool, proj_done, 24 * l + 30, "pool")
                    load_cache(l, s, s, 1)
                hold(pool, qkv_done, l + 1, "pool")
                kvn = proj[:, :, K0:K0 + 2 * AW].rearrange("p i (k n) -> p i k n", k=2)
                out_p = [io["kvp128"], io["kvp512"], io["kvp2048"]]
                out_s = [io["kvs128"], io["kvs512"], io["kvs2048"]]
                for g, (win, _) in enumerate(GROUPS):
                    cols = slice(g * P, g * P + P)
                    for i in range(2):
                        if min(win, SEQ) == SEQ or i == 1:
                            r0 = i * P if min(win, SEQ) == SEQ else 0
                            pool.dma_start(out_p[g].rearrange("l b r k h d -> l b r k (h d)")[l, 0, r0:r0 + P],
                                           kvn[:, i, :, cols]).then_inc(rows_out, 16)
                    for t in range(NT):
                        pool.dma_start(out_s[g].rearrange("l b r k h d -> l b r k (h d)")[l, :, win - NT + t],
                                       kvn[t:NS:NT, 2, :, cols]).then_inc(rows_out, 16)
                pool.dma_start(io["conv_prompt"][l, 0], proj[P - 2:P, 1, XB0:XB0 + BW]).then_inc(rows_out, 16)
                for j in range(2):
                    pool.dma_start(io["conv_sample"][l, :, j], proj[NT - 2 + j:NS:NT, 2, XB0:XB0 + BW]).then_inc(rows_out, 16)
                pool.dma_start(io["chunk_v"].rearrange("l b t h d -> l (b t) (h d)")[l],
                               proj[0:NS, 2, CV0:CV0 + CW]).then_inc(rows_out, 16)
                hold(pool, pv_done, l + 1, "pool")
                hold(pool, rows_out, 16 * N_ROWS * (l + 1), "pool")
                for p, (i, h0, h1) in enumerate(PARTS[:6]):
                    if i < 2:
                        hold(pool, route_done, NP * l + p + 1, "pool")
                        lo, hi = h0 * TOP // BATCH // 2, h1 * TOP // BATCH // 2
                    else:
                        hold(pool, idxrep_loaded, 128 * (l + 1), "pool")
                        lo, hi = 0, BATCHES[2] // 2
                    with pool.Fori(lo, hi) as c:
                        for s in range(2):
                            n = ALL_B * l + BASE[i] + 2 * c + s
                            hold(pool, v_used, BATCH * n + BATCH, "pool")
                            pool.tensor_copy(stage[:, s, :], idx[:, bass.ds(COL0[i] + (2 * c + s) * BATCH, BATCH)]).then_inc(staged, 1)
                            hold(pool, staged, n + 1, "pool")
                            for k in range(BATCH):
                                hold(pool, dot_done, BATCH * n + k + 1, "pool")
                                pool.indirect_dma_start(
                                    out=urow[:, k, :], out_offset=None, in_=io["peer_u"].rearrange("l e d -> (l e) d"),
                                    in_offset=bass.IndirectOffsetOnAxis(ap=stage[:, s, k:k + 1], axis=0)).then_inc(u_in[k], 16)
                            for k in range(BATCH):
                                hold(pool, v_used, BATCH * n + BATCH + k + 1, "pool")
                                pool.indirect_dma_start(
                                    out=vrow[:, k, :], out_offset=None, in_=io["peer_v"].rearrange("l e d -> (l e) d"),
                                    in_offset=bass.IndirectOffsetOnAxis(ap=stage[:, s, k:k + 1], axis=0)).then_inc(v_in[k], 16)

        @block.scalar
        def _(a):
            a.wait_ge(x_loaded, 32)
            a.sem_inc(x_done, 3)
            for h in range(HEADS):
                a.wait_ge(bias_ps, h + 1)
                last = a.activation(wide[:, h, :], bank[h][:, 0:PITCH], ACT.Copy)
            last.then_inc(bias_wide, 1)

            def norm(l, which):
                for i in range(TILES):
                    last = a.activation(xn[:, i, :], x[:, i, :], ACT.Square, accum_out=ssq[:, i:i + 1])
                last.then_inc(square_sum, 1)
                a.wait_ge(rms_mean, 2 * l + which + 1)
                a.activation(ssq[:, :], ssq[:, :], ACT.Sqrt).then_inc(rms_root, 1)
                for j in range(2 * TILES):
                    i, half = j // 2, j % 2
                    hold(a, xt_ps, 12 * l + 6 * which + j + 1, "act")
                    a.activation(xt[:, 4 * half:4 * half + 4, T0[i]:T0[i] + ROWS[i]],
                                 bank[j][:, :].rearrange("p (c n) -> p c n", c=4)[:, :, 0:ROWS[i]], ACT.Copy).then_inc(xt_done, 1)

            def exps(l, slot, n, rows, logits):
                a.wait_ge(max_done, 3 * l + slot + 1)
                a.activation(share[0:rows, :], dmax[0:rows, :], ACT.Exp)
                for h in range(HEADS):
                    last = a.activation(logits[0:rows, h, 0:n], logits[0:rows, h, 0:n], ACT.Exp,
                                        bias=nmax[0:rows, h:h + 1], accum_out=esum[0:rows, h:h + 1])
                last.then_inc(exp_done, 1)

            def batches(l, i, lo, hi):
                with a.Fori(lo // 2, hi // 2) as c:
                    for s in range(2):
                        n = ALL_B * l + BASE[i] + 2 * c + s
                        a.wait_ge(dot_done, BATCH * n + 2 * BATCH)
                        a.activation(act[:, s, :], hid[:, s, :], ACT.Gelu_apprx_tanh).then_inc(act_done, 1)

            def score_copy(l, p):
                i, h0, h1 = PARTS[p]
                a.wait_ge(score_ps, NP * l + p + 1)
                r = ROWS[i]
                for j in range((h1 - h0) // 2):
                    c0 = 256 * h0 + 512 * j
                    last = a.activation(scores[0:r, c0:c0 + 512], bank[score_bank(p) + j][0:r, :], ACT.Copy)
                last.then_inc(score_done, 1)

            def gate_exp(l, p):
                i, h0, h1 = PARTS[p]
                hold(a, pick_done, NP * l + p + 1, "act")
                a.activation(ts[0:ROWS[i], h0:h1, :], ts[0:ROWS[i], h0:h1, :], ACT.Exp).then_inc(gexp_done, 1)

            def y_copy(l, i):
                b0 = 4 + 2 * (i % 2)
                a.wait_ge(y_ps, 3 * l + i + 1)
                for half in range(2):
                    last = a.activation(x[:, i, 512 * half:512 * half + 512], bank[b0 + half][:, :], ACT.Copy)
                last.then_inc(x_done, 1)

            with a.Fori(0, DEPTH) as l:
                hold(a, x_done, 3 * l + 3, "act")
                norm(l, 0)
                hold(a, prep_ps, l + 1, "act")
                a.activation(wmt[:, 0:4, :], bank[6][:, :].rearrange("p (h n) -> p h n", h=4), ACT.Copy)
                a.activation(wmt[:, 4, :], bank[7][:, 0:P], ACT.Copy)
                a.activation(bst[:, :], bank[7][:, P:P + CH], ACT.Copy)
                a.activation(cwt[:, 0:2, :], bank[7][:, 136:142].rearrange("p (c j) -> p c j", c=2), ACT.Copy)
                a.activation(cwt[0:64, 2, :], bank[7][0:64, 142:145], ACT.Copy)
                a.activation(zs[:, 0:2, :, 0:2], bank[7][:, 160:192].rearrange("p (c b j) -> p c b j", c=2, b=NB), ACT.Copy)
                a.activation(zs[0:64, 2, :, 0:2], bank[7][0:64, 192:208].rearrange("p (b j) -> p b j", b=NB), ACT.Copy).then_inc(prep_done, 1)
                def proj_copy(lo, hi):
                    with a.Fori(lo, hi) as c:
                        for s in range(2):
                            for i in range(TILES):
                                hold(a, proj_ps, 24 * l + 6 * c + 3 * s + i + 1, "act")
                                a.activation(proj[0:ROWS[i], i, bass.ds((2 * c + s) * W_IN, W_IN)],
                                             bank[3 * s + i][0:ROWS[i], 0:W_IN], ACT.Copy).then_inc(proj_done, 1)
                    a.drain()

                a.wait_ge(skew_written, 16)
                proj_copy(0, 1)
                a.activation(sqk[0:NS, 2, 0:AW], proj[0:NS, 2, Q0:Q0 + AW], ACT.Square).then_inc(q_square, 1)
                hold(a, q_mean, l + 1, "act")
                a.activation(qss[:, :], qss[:, :], ACT.Sqrt).then_inc(q_root, 1)
                proj_copy(1, N_IN // 2)
                for i in range(TILES):
                    r = ROWS[i]
                    c0 = 0 if i < 2 else AW
                    last = a.activation(sqk[0:r, i, c0:], proj[0:r, i, c0:2 * AW], ACT.Square)
                last.then_inc(squares, 1)
                for i in range(TILES):
                    r = ROWS[i]
                    a.activation(proj[0:r, i, U0:U0 + 2 * CW], proj[0:r, i, U0:U0 + 2 * CW], ACT.Gelu_apprx_tanh)
                a.drain()
                for i in range(TILES):
                    r = ROWS[i]
                    last = a.activation(sqv[0:r, i, :], proj[0:r, i, CV0:CV0 + CW], ACT.Square)
                last.then_inc(squares, 1)
                for i in range(TILES):
                    r, t0, bz, bg = ROWS[i], T0[i], bank[2 * i], bank[2 * i + 1]
                    hold(a, zg_ps, 3 * l + i + 1, "act")
                    gv = bg[:, 0:384].rearrange("p (c n) -> p c n", c=3)
                    zv = bz[:, 0:384].rearrange("p (c n) -> p c n", c=3)
                    a.activation(gt[:, 0:2, t0:t0 + r], gv[:, 0:2, 0:r], ACT.Copy)
                    a.activation(gt[0:64, 2, t0:t0 + r], gv[0:64, 2, 0:r], ACT.Copy)
                    if i < 2:
                        a.activation(zt[:, 0:2, 2 + t0:2 + t0 + r], zv[:, 0:2, 0:r], ACT.Copy)
                        a.activation(zt[0:64, 2, 2 + t0:2 + t0 + r], zv[0:64, 2, 0:r], ACT.Copy).then_inc(zg_done, 1)
                    else:
                        for ch in range(3):
                            w = 128 if ch < 2 else 64
                            last = a.activation(zs[0:w, ch, :, 2:6], zv[0:w, ch, 0:r].rearrange("p (b t) -> p b t", b=NB), ACT.Copy)
                        last.then_inc(zg_done, 1)
                hold(a, head_mean, l + 1, "act")
                a.activation(hss[:, :, :], hss[:, :, :], ACT.Sqrt).then_inc(head_root, 1)
                for i in range(TILES):
                    r, t0 = ROWS[i], T0[i]
                    hold(a, yct_ps, 3 * l + i + 1, "act")
                    v = bank[2 * i][:, 0:384].rearrange("p (c n) -> p c n", c=3)
                    a.activation(yt[64:128, 5, t0:t0 + r], v[64:128, 0, 0:r], ACT.Copy)
                    a.activation(yt[:, 6:8, t0:t0 + r], v[:, 1:3, 0:r], ACT.Copy).then_inc(yct_done, 1)
                for j in range(2 * TILES):
                    i = j // 2
                    r, t0 = ROWS[i], T0[i]
                    hold(a, qkt_ps, 6 * l + j + 1, "act")
                    v = bank[1 + 2 * (j % 4)][:, 0:384].rearrange("p (c n) -> p c n", c=3)
                    a.activation((kt if j % 2 else qt)[:, :, t0:t0 + r], v[:, :, 0:r], ACT.Copy).then_inc(qkt_done, 1)
                exps(l, 0, P + NS, NS, lgs)
                hold(a, probt_ps, 3 * l + 1, "act")
                a.activation(pts[:, :, :], pts_ps, ACT.Copy)
                a.activation(pte[0:NS, :, :], pte_ps[0:NS], ACT.Copy).then_inc(probt_done, 1)
                hold(a, pnew_ps, l + 1, "act")
                a.activation(pnew[:, :, :], pnew_sum, ACT.Copy).then_inc(pnew_done, 1)
                for slot, q in ((1, 1), (2, 0)):
                    exps(l, slot, P * (q + 1), P, lgp[:, q])
                for slot, q in ((1, 1), (2, 0)):
                    hold(a, probt_ps, 3 * l + slot + 1, "act")
                    blocks = HEADS * (q + 1)
                    for j, b in enumerate(prob_banks[q]):
                        k = min(4, blocks - 4 * j)
                        last = a.activation((pt0 if q == 0 else pt1)[:, 4 * j:4 * j + k, :],
                                            b[:, 0:k * P].rearrange("p (s n) -> p s n", s=k), ACT.Copy)
                    last.then_inc(probt_done, 1)
                    hold(a, ya_ps, 2 * l + slot, "act")
                    a.activation(yt[:, 0:3, q * P:q * P + P],
                                 ya_bank[q][:, 0:384].rearrange("p (g n) -> p g n", g=NG), ACT.Copy).then_inc(ya_done, 1)
                hold(a, h_done, 12 * l + 24, "act")
                norm(l, 1)
                hold(a, keyt_ps, l + 1, "act")
                a.activation(ktt[:, :, :], bank[6][:, 0:256].rearrange("p (j n) -> p j n", j=2), ACT.Copy).then_inc(keyt_done, 1)
                def qf_copy(lo, hi):
                    with a.Fori(lo, hi) as c:
                        for s in range(2):
                            for j in range(2):
                                hold(a, qf_ps, 16 * l + 4 * c + 2 * s + j + 1, "act")
                                a.activation(qf[:, bass.ds(4 * c + 2 * s + j, 1), :], bank[2 * s + j][:, 0:TOKENS].unsqueeze(1), ACT.Copy).then_inc(qf_done, 1)

                qf_copy(0, 1)
                score_copy(l, 0)
                qf_copy(1, 2)
                score_copy(l, 1)
                gate_exp(l, 0)
                qf_copy(2, 3)
                gate_exp(l, 1)
                qf_copy(3, 4)
                score_copy(l, 2)
                batches(l, 0, 0, 2)
                gate_exp(l, 2)
                a.wait_ge(route_done, NP * l + 3)
                score_copy(l, 3)
                score_copy(l, 4)
                batches(l, 0, 2, 6)
                gate_exp(l, 3)
                batches(l, 0, 6, 10)
                gate_exp(l, 4)
                a.wait_ge(route_done, NP * l + 5)
                score_copy(l, 5)
                score_copy(l, 6)
                batches(l, 0, 10, 14)
                gate_exp(l, 5)
                batches(l, 0, 14, 16)
                y_copy(l, 0)
                batches(l, 1, 0, 2)
                gate_exp(l, 6)
                batches(l, 1, 2, 16)
                y_copy(l, 1)
                batches(l, 2, 0, 4)
                y_copy(l, 2)

        @block.vector
        def _(v):
            v.memset(relb[N_BUCKETS:N_BUCKETS + 1, :], 1.0)
            v.memset(wss[:, :, :], 0.0).then_inc(wss_clear, 1)
            v.memset(hss[:, :, :], 1.0)
            v.memset(layer0[:, :], 0.0)
            v.drain()
            v.wait_ge(const_loaded, 112)
            v.tensor_copy(relw, relb[:, :].unsqueeze(2).broadcast_to([N_BUCKETS + 1, HEADS, P]))
            v.tensor_tensor(relt, relb[:, :].unsqueeze(2).broadcast_to([N_BUCKETS + 1, HEADS, P]),
                            cturn.unsqueeze(1).broadcast_to([N_BUCKETS + 1, HEADS, P]), ALU.mult).then_inc(rel_ready, 1)
            v.wait_ge(bias_ps, HEADS + 1)
            for j in range(2):
                last = v.tensor_tensor(sbias[:, 3 * j:3 * j + 3, :],
                                       bank[6 + j][0:NS, 0:480].rearrange("p (h n) -> p h n", h=3),
                                       cother.unsqueeze(1).broadcast_to([NS, 3, P + NS]), ALU.add)
            last.then_inc(bias_sample, 1)

            def norm(l, which):
                v.wait_ge(square_sum, 2 * l + which + 1)
                v.tensor_scalar(ssq[:, :], ssq[:, :], 1.0 / D, EPS, ALU.mult, ALU.add).then_inc(rms_mean, 1)
                v.wait_ge(rms_root, 2 * l + which + 1)
                v.reciprocal(ssq[:, :], ssq[:, :])
                v.drain()
                hold(v, gain_loaded, 32 * l + 16 * which + 16, "dve")
                for i in range(TILES):
                    v.scalar_tensor_tensor(out=xn[:, i, :], in0=x[:, i, :], scalar=ssq[:, i:i + 1], in1=gain[:, :],
                                           op0=ALU.mult, op1=ALU.mult).then_inc(xn_done, 1)

            def softmax(l, slot, n, rows, logits):
                lg = logits[0:rows, :, 0:n]
                v.drain()
                v.tensor_reduce(nmax[0:rows, :], lg, AX.X, ALU.max, negate=True)
                v.drain()
                by_head = nmax[0:rows, :].rearrange("p (g h) -> p h g", h=2)
                v.tensor_reduce(nall[0:rows, :], by_head, AX.X, ALU.min)
                v.drain()
                v.tensor_tensor(dmax[0:rows, :].rearrange("p (g h) -> p g h", h=2),
                                nall[0:rows, :].unsqueeze(1).broadcast_to([rows, NG, 2]),
                                nmax[0:rows, :].rearrange("p (g h) -> p g h", h=2), ALU.subtract).then_inc(max_done, 1)
                v.wait_ge(exp_done, 3 * l + slot + 1)
                v.tensor_tensor(part[0:rows, :], esum[0:rows, :], share[0:rows, :], ALU.mult)
                v.drain()
                v.tensor_reduce(total[0:rows, :], part[0:rows, :].rearrange("p (g h) -> p h g", h=2), AX.X, ALU.add)
                v.drain()
                v.reciprocal(total[0:rows, :], total[0:rows, :])
                v.drain()
                v.tensor_tensor(part[0:rows, :].rearrange("p (g h) -> p g h", h=2),
                                share[0:rows, :].rearrange("p (g h) -> p g h", h=2),
                                total[0:rows, :].unsqueeze(1).broadcast_to([rows, NG, 2]), ALU.mult)
                v.drain()
                v.tensor_tensor(lg, lg, part[0:rows, :].unsqueeze(2).broadcast_to([rows, HEADS, n]), ALU.mult).then_inc(prob_done, 1)

            def route(l, p):
                i, h0, h1 = PARTS[p]
                r = ROWS[i]
                hh, jj = h1 - h0, 2 * (h1 - h0)
                c0, c1 = 256 * h0, 256 * h1
                s3 = scores[0:r, c0:c1].rearrange("p (j n) -> p j n", j=jj)
                c3 = cand[0:r, c0:c1].rearrange("p (j n) -> p j n", j=jj)
                top_, topi_, topf_ = (b[0:r, 2 * h0:2 * h1, :] for b in (top, topi, topf))
                ts_, ti_ = (b[0:r, h0:h1, :] for b in (ts, ti))
                ps = slice(TOP * h0, TOP * h1)
                picks = hh * TOP
                v.drain()
                hold(v, score_done, NP * l + p + 1, "dve")
                for j in range(jj):
                    v.max(top_[:, j, 0:8], s3[:, j, :])
                v.drain()
                for j in range(jj):
                    v.max_index(topi_[:, j, 0:8], top_[:, j, 0:8], s3[:, j, :])
                    v.match_replace(c3[:, j, :], top_[:, j, 0:8], s3[:, j, :], LOW)
                v.drain()
                for j in range(jj):
                    v.max(top_[:, j, 8:16], c3[:, j, :])
                v.drain()
                for j in range(jj):
                    v.max_index(topi_[:, j, 8:16], top_[:, j, 8:16], c3[:, j, :])
                v.drain()
                v.tensor_copy(topf_, topi_)
                t4 = top_.rearrange("p (h s) k -> p h s k", s=2)
                pair = cand[0:r, c0:c1].rearrange("p (h a b) -> p h a b", h=hh, a=TOP)
                for h in range(hh):
                    v.tensor_tensor(pair[:, h], t4[:, h, 0, :].unsqueeze(2).broadcast_to([r, TOP, TOP]),
                                    t4[:, h, 1, :].unsqueeze(1).broadcast_to([r, TOP, TOP]), ALU.add)
                v.drain()
                p3 = cand[0:r, c0:c1].rearrange("p (h n) -> p h n", h=hh)
                q3 = scores[0:r, c0:c1].rearrange("p (h n) -> p h n", h=hh)
                for h in range(hh):
                    v.max(ts_[:, h, 0:8], p3[:, h, :])
                v.drain()
                for h in range(hh):
                    v.max_index(ti_[:, h, 0:8], ts_[:, h, 0:8], p3[:, h, :])
                    v.match_replace(q3[:, h, :], ts_[:, h, 0:8], p3[:, h, :], LOW)
                v.drain()
                for h in range(hh):
                    v.max(ts_[:, h, 8:16], q3[:, h, :])
                v.drain()
                for h in range(hh):
                    v.max_index(ti_[:, h, 8:16], ts_[:, h, 8:16], q3[:, h, :])
                v.tensor_copy(gmax[0:r, 0:hh], ts_[:, :, 0])
                v.drain()
                v.tensor_tensor(ts_, ts_, gmax[0:r, 0:hh].unsqueeze(2).broadcast_to([r, hh, TOP]), ALU.subtract).then_inc(pick_done, 1)
                tif = ti_.rearrange("p h k -> p (h k)")
                v.tensor_scalar(tab[0:r, 0, ps], tif, 4, None, ALU.logical_shift_right)
                v.tensor_scalar(tab[0:r, 1, ps], tif, 15, None, ALU.bitwise_and)
                v.drain()
                v.tensor_copy(tabf[0:r, :, ps], tab[0:r, :, ps])
                v.drain()
                f4 = topf_.rearrange("p (h s) k -> p h s k", s=2)
                for key, buf in ((0, scores), (1, cand)):
                    hot = buf[0:r, c0:c1].rearrange("p (n a) -> p n a", a=TOP)
                    v.tensor_tensor(hot, sixteen[0:r, :].unsqueeze(1).broadcast_to([r, picks, TOP]),
                                    tabf[0:r, key, ps].unsqueeze(2).broadcast_to([r, picks, TOP]), ALU.is_equal)
                v.drain()
                for key, buf in ((0, scores), (1, cand)):
                    hot = buf[0:r, c0:c1].rearrange("p (h k a) -> p h k a", h=hh, k=TOP)
                    for h in range(hh):
                        v.tensor_tensor(hot[:, h], hot[:, h], f4[:, h, key, :].unsqueeze(1).broadcast_to([r, TOP, TOP]), ALU.mult)
                v.drain()
                for key, buf in ((0, scores), (1, cand)):
                    v.tensor_reduce(pos[0:r, key, ps], buf[0:r, c0:c1].rearrange("p (n a) -> p n a", a=TOP), AX.X, ALU.add)
                v.drain()
                v.scalar_tensor_tensor(out=eidx[0:r, ps], in0=pos[0:r, 0, ps], scalar=float(NK), in1=pos[0:r, 1, ps],
                                       op0=ALU.mult, op1=ALU.add)
                v.drain()
                cols = slice(COL0[i] + ps.start, COL0[i] + ps.stop) if i < 2 else ps
                to_i, to_g = (idx[:, cols], gate[:, cols]) if i < 2 else (idx2[:, cols], gate2[:, cols])
                v.tensor_scalar(to_i, eidx[0:r, ps], layer0[0:r, :], None, ALU.add)
                hold(v, gexp_done, NP * l + p + 1, "dve")
                v.tensor_reduce(gsum[0:r, 0:hh], ts_, AX.X, ALU.add)
                v.drain()
                v.reciprocal(gsum[0:r, 0:hh], gsum[0:r, 0:hh])
                v.drain()
                v.tensor_tensor(to_g.rearrange("p (h k) -> p h k", h=hh), ts_,
                                gsum[0:r, 0:hh].unsqueeze(2).broadcast_to([r, hh, TOP]), ALU.mult).then_inc(route_done, 1)

            def batches(l, i, lo, hi):
                mask = ident2[:, 0 if i < 2 else 1, :]
                with v.Fori(lo // 2, hi // 2) as c:
                    for s in range(2):
                        n = ALL_B * l + BASE[i] + 2 * c + s
                        for k in range(BATCH):
                            v.wait_ge(u_in[k], 16 * n + 16)
                            v.scalar_tensor_tensor(out=urow[:, k, :], in0=urow[:, k, :], scalar=1.0, in1=xn[:, i, :],
                                                   op0=ALU.mult, op1=ALU.mult, accum_out=hid[:, s, k:k + 1]).then_inc(dot_done, 1)
                        hold(v, v_used, BATCH * n + BATCH, "dve")
                        hold(v, act_done, n + 1, "dve")
                        for k in range(BATCH):
                            last = v.tensor_scalar(diag[:, s, k, :], mask, act[:, s, k:k + 1],
                                                   gate[:, bass.ds(COL0[i] + (2 * c + s) * BATCH + k, 1)], ALU.mult, ALU.mult)
                        last.then_inc(diag_done, 1)

            with v.Fori(0, DEPTH) as l:
                norm(l, 0)
                hold(v, q_square, l + 1, "dve")
                v.tensor_reduce(qss[:, :], sqk[0:NS, 2, 0:AW].rearrange("p (h d) -> p h d", d=HD), AX.X, ALU.add)
                v.drain()
                v.tensor_scalar(qss[:, :], qss[:, :], 1.0 / HD, EPS, ALU.mult, ALU.add).then_inc(q_mean, 1)
                hold(v, q_root, l + 1, "dve")
                v.reciprocal(qss[:, :], qss[:, :])
                v.drain()
                qs = proj[0:NS, 2, Q0:Q0 + AW].rearrange("p (h d) -> p h d", d=HD)
                v.tensor_tensor(qs, qs, qss[:, :].unsqueeze(2).broadcast_to([NS, HEADS, HD]), ALU.mult)
                v.drain()
                hold(v, small_loaded, 112 * (l + 1), "dve")
                v.tensor_tensor(qs, qs, gqk[0:NS, 0, :].unsqueeze(1).broadcast_to([NS, HEADS, HD]), ALU.mult).then_inc(q_ready, 1)
                with v.Fori(0, NB // 2) as c:
                    for s in range(2):
                        b = 2 * c + s
                        hold(v, cache_in[s], 304 * l + 64 * (c + 1), "dve")
                        for t in range(NT):
                            v.tensor_tensor(kq[:, t, P:3 * P].rearrange("p (g n) -> p g n", g=2), qbs[s][:, t, P:3 * P].rearrange("p (g n) -> p g n", g=2),
                                            ckv[:, s, t:8:4, :], ALU.mult)
                            last = v.tensor_tensor(kq[:, t, 0:P], qbs[s][:, t, 0:P], ckv[:, s, 8, :], ALU.mult)
                        last.then_inc(kq_done, 1)
                        v.drain()
                        v.tensor_reduce(lgt[:, :, bass.ds(b * NT, NT)].rearrange("p h t -> p t h"),
                                        kq[:, :, :].rearrange("p t (h d) -> p t h d", d=HD), AX.X, ALU.add)
                        v.drain()
                v.drain().then_inc(kq_summed, 1)
                hold(v, squares, 2 * l + 1, "dve")
                for i in range(TILES):
                    r = ROWS[i]
                    last = v.tensor_tensor(proj[0:r, i, XB0:XB0 + BW], proj[0:r, i, GC0:GC0 + BW], proj[0:r, i, XB0:XB0 + BW], ALU.mult)
                last.then_inc(zb_done, 1)
                for i in range(TILES):
                    r = ROWS[i]
                    h0 = 0 if i < 2 else HEADS
                    v.tensor_reduce(hss[0:r, i, h0:2 * HEADS], sqk[0:r, i, h0 * HD:].rearrange("p (h d) -> p h d", d=HD), AX.X, ALU.add)
                hold(v, squares, 2 * l + 2, "dve")
                for i in range(TILES):
                    r = ROWS[i]
                    v.tensor_reduce(hss[0:r, i, 2 * HEADS:], sqv[0:r, i, :].rearrange("p (h d) -> p h d", d=HD), AX.X, ALU.add)
                v.drain()
                v.tensor_scalar(hss[:, :, :], hss[:, :, :], 1.0 / HD, EPS, ALU.mult, ALU.add).then_inc(head_mean, 1)
                hold(v, head_root, l + 1, "dve")
                v.reciprocal(hss[:, :, :], hss[:, :, :])
                v.drain()
                for i in range(TILES):
                    r = ROWS[i]
                    h0 = 0 if i < 2 else HEADS
                    qk = proj[0:r, i, h0 * HD:2 * AW].rearrange("p (h d) -> p h d", d=HD)
                    vc = proj[0:r, i, CV0:CV0 + CW].rearrange("p (h d) -> p h d", d=HD)
                    v.tensor_tensor(vc, vc, hss[0:r, i, 2 * HEADS:].unsqueeze(2).broadcast_to([r, CH, HD]), ALU.mult)
                    v.tensor_tensor(qk, qk, hss[0:r, i, h0:2 * HEADS].unsqueeze(2).broadcast_to([r, 2 * HEADS - h0, HD]), ALU.mult)
                v.drain()
                for i in range(TILES):
                    r = ROWS[i]
                    vc = proj[0:r, i, CV0:CV0 + CW]
                    v.tensor_tensor(vc, vc, gcv[0:r, :], ALU.mult)
                    for j in range(0 if i < 2 else 1, 2):
                        qk = proj[0:r, i, j * AW:(j + 1) * AW].rearrange("p (h d) -> p h d", d=HD)
                        last = v.tensor_tensor(qk, qk, gqk[0:r, j, :].unsqueeze(1).broadcast_to([r, HEADS, HD]), ALU.mult)
                last.then_inc(qkv_done, 1)
                v.memset(zt[:, :, 0:2], 0.0)
                for i in range(TILES):
                    v.memset(ycm[:, i, 0:64], 0.0)
                v.drain()
                hold(v, zg_done, 3 * l + 3, "dve")
                for j in range(3):
                    for ch in range(3):
                        w = 128 if ch < 2 else 64
                        tap = cwt[0:w, ch, j:j + 1]
                        for src, dst in ((zt[0:w, ch, j:j + SEQ], acc[0:w, ch, 0:SEQ]),
                                         (zs[0:w, ch, :, j:j + NT], acc[0:w, ch, SEQ:TOKENS].rearrange("p (b t) -> p b t", b=NB))):
                            if j == 0:
                                v.tensor_scalar(dst, src, tap, None, ALU.mult)
                            else:
                                v.scalar_tensor_tensor(out=dst, in0=src, scalar=tap, in1=dst, op0=ALU.mult, op1=ALU.add)
                    v.drain()
                v.tensor_tensor(yt[:, 3:5, :], acc[:, 0:2, :], gt[:, 0:2, :], ALU.mult)
                v.tensor_tensor(yt[0:64, 5, :], acc[0:64, 2, :], gt[0:64, 2, :], ALU.mult).then_inc(yb_done, 1)
                hold(v, cblock_loaded, 256 * (l + 1), "dve")
                for i in range(TILES):
                    r = ROWS[i]
                    bs = (bst if i < 2 else bss)[0:r, :]
                    hold(v, mix_ps, 3 * l + i + 1, "dve")
                    mixed = ycm[0:r, i, 64:64 + CW]
                    v.tensor_tensor(mixed.rearrange("p (h d) -> p h d", d=HD),
                                    bank[6 + i % 2][0:r, 0:CW].rearrange("p (h d) -> p h d", d=HD),
                                    bs.unsqueeze(2).broadcast_to([r, CH, HD]), ALU.add)
                    v.drain()
                    v.tensor_tensor(mixed, mixed, proj[0:r, i, U0:U0 + CW], ALU.mult).then_inc(yc_done, 1)
                hold(v, logit_ps, 3 * l + 1, "dve")
                for j in range(2):
                    v.scalar_tensor_tensor(out=lgs[0:NS, 3 * j:3 * j + 3, 0:P], in0=old_ps[j],
                                           scalar=SCALE, in1=sbias[:, 3 * j:3 * j + 3, 0:P], op0=ALU.mult, op1=ALU.add)
                    v.scalar_tensor_tensor(out=lgs[0:NS, j:HEADS:2, P:P + NS], in0=new_ps[j],
                                           scalar=SCALE, in1=sbias[:, j:HEADS:2, P:P + NS], op0=ALU.mult, op1=ALU.add)
                softmax(l, 0, P + NS, NS, lgs)
                v.wait_ge(toep_loaded, 16)
                for slot, q in ((1, 1), (2, 0)):
                    n = P * (q + 1)
                    hold(v, logit_ps, 3 * l + slot + 1, "dve")
                    for heads, b in lg_ps[q]:
                        k = len(heads)
                        hs = slice(heads[0], heads[-1] + 1, 2)
                        v.scalar_tensor_tensor(out=lgp[:, q, hs, 0:n], in0=b[:, 0:k * n].rearrange("p (h n) -> p h n", h=k),
                                               scalar=SCALE, in1=toep[:, hs, 2 * P - n:2 * P], op0=ALU.mult, op1=ALU.add)
                    softmax(l, slot, n, P, lgp[:, q])
                hold(v, pnew_done, l + 1, "dve")
                hold(v, pv_done, l + 1, "dve")
                for h in range(2):
                    r = slice(64 * h, 64 * h + 64)
                    last = v.tensor_tensor(yt[r, 0:3, SEQ:TOKENS], pv_sum[r, :, h, :], pnew[r, :, :], ALU.add)
                last.then_inc(yas_done, 1)
                with v.Fori(0, N_OUT // 2) as c:
                    for s in range(2):
                        for i in range(TILES):
                            r = ROWS[i]
                            v.wait_ge(h_ps, 12 * l + 6 * c + 3 * s + i + 1)
                            xs = x[0:r, i, bass.ds((2 * c + s) * W_OUT, W_OUT)]
                            v.tensor_tensor(xs, bank[3 * s + i][0:r, 0:W_OUT], xs, ALU.add).then_inc(h_done, 1)
                norm(l, 1)
                route(l, 0)
                route(l, 1)
                batches(l, 0, 0, 2)
                route(l, 2)
                batches(l, 0, 2, 6)
                route(l, 3)
                batches(l, 0, 6, 10)
                route(l, 4)
                batches(l, 0, 10, 14)
                route(l, 5)
                batches(l, 0, 14, 16)
                batches(l, 1, 0, 2)
                route(l, 6)
                batches(l, 1, 2, 16)
                hold(v, xrep_loaded, 48 * (l + 1), "dve")
                hold(v, idxrep_loaded, 128 * (l + 1), "dve")
                batches(l, 2, 0, 4)
                v.tensor_scalar(layer0[:, :], layer0[:, :], float(NE), None, ALU.add)

        @block.tensor
        def _(pe):
            pe.wait_ge(rel_ready, 1)
            for h in range(HEADS):
                pe.matmul(bank[h][:, 0:PITCH], relw[:, h, :], cprompt[:, h // 2, :], start=True, stop=True).then_inc(bias_ps, 1)
            for h in range(HEADS):
                o = bank[6 + h // 3][0:NS, (h % 3) * 160:(h % 3) * 160 + 160]
                for t in range(NT):
                    last = pe.matmul(o, relt[:, h, t * NS:t * NS + NS], csample[:, h // 2, t, :], start=(t == 0), stop=(t == NT - 1))
            last.then_inc(bias_ps, 1)
            pe.wait_ge(bias_sample, 1)
            pe.wait_ge(bias_wide, 1)

            def norm_t(l, which):
                for j in range(2 * TILES):
                    i, half = j // 2, j % 2
                    r = ROWS[i]
                    if half == 0:
                        hold(pe, xn_done, 6 * l + 3 * which + i + 1, "pe")
                    for c in range(4):
                        last = pe.transpose(bank[j][:, c * P:c * P + r], xn[0:r, i, (4 * half + c) * P:(4 * half + c + 1) * P], ident[0:r, 0:r])
                    last.then_inc(xt_ps, 1)
                hold(pe, xt_done, 12 * l + 6 * which + 6, "pe")

            def score(l, p):
                i, h0, h1 = PARTS[p]
                r = ROWS[i]
                for j in range(2 * (h1 - h0)):
                    last = pe.matmul(bank[score_bank(p) + j // 4][0:r, (j % 4) * P:(j % 4 + 1) * P], qf[:, 2 * h0 + j, T0[i]:T0[i] + r], ktt[:, j % 2, :],
                                     start=True, stop=True)
                last.then_inc(score_ps, 1)

            def open_y(l, i):
                b0 = 4 + 2 * (i % 2)
                if i == 2:
                    hold(pe, x_done, 3 * l + 4, "pe")
                for half in range(2):
                    pe.matmul(bank[b0 + half][:, :], ident[0:64, :], x[0:64, i, 512 * half:512 * half + 512], start=True, stop=False)

            def batches(l, i, lo, hi):
                b0 = 4 + 2 * (i % 2)
                with pe.Fori(lo // 2, hi // 2) as c:
                    for s in range(2):
                        n = ALL_B * l + BASE[i] + 2 * c + s
                        hold(pe, diag_done, n + 1, "pe")
                        for k in range(BATCH):
                            hold(pe, v_in[k], 16 * n + 16, "pe")
                            for half in range(2):
                                last = pe.matmul(bank[b0 + half][:, :], diag[:, s, k, :], vrow[:, k, 512 * half:512 * half + 512], start=False, stop=False)
                            last.then_inc(v_used, 1)

            def close_y(l, i):
                b0 = 4 + 2 * (i % 2)
                for half in range(2):
                    last = pe.matmul(bank[b0 + half][:, :], ident[64:128, :], x[64:128, i, 512 * half:512 * half + 512], start=False, stop=True)
                last.then_inc(y_ps, 1)

            with pe.Fori(0, DEPTH) as l:
                norm_t(l, 0)
                hold(pe, small_loaded, 112 * (l + 1), "pe")
                for h in range(CH):
                    pe.transpose(bank[6 + h // 4][:, (h % 4) * P:(h % 4 + 1) * P], cws[:, h, :], ident)
                pe.transpose(bank[7][:, P:P + CH], brow[:, :], ident[0:CH, 0:CH])
                for ch in range(3):
                    w = 128 if ch < 2 else 64
                    pe.transpose(bank[7][0:w, 136 + 3 * ch:139 + 3 * ch], crow[:, ch * P:ch * P + w], ident[0:3, 0:3])
                    last = pe.transpose(bank[7][0:w, 160 + 16 * ch:176 + 16 * ch], srow[:, ch * P:ch * P + w], ident[0:2 * NB, 0:2 * NB])
                last.then_inc(prep_ps, 1)
                with pe.Fori(0, N_IN // 2) as c:
                    for s in range(2):
                        w = wring[:, s, 0:KCH * W_IN].rearrange("p (k n) -> p k n", k=KCH)
                        hold(pe, w_loaded[s], 16 * (N_W // 2 * l + c + 1), "pe")
                        for i in range(TILES):
                            hold(pe, proj_done, 24 * l + 6 * c + 3 * s + i + 1, "pe")
                            for k in range(KCH):
                                last = pe.matmul(bank[3 * s + i][0:ROWS[i], 0:W_IN], xt[:, k, T0[i]:T0[i] + ROWS[i]], w[:, k, :],
                                                 start=(k == 0), stop=(k == KCH - 1))
                            last.then_inc(proj_ps, 1)
                hold(pe, zb_done, l + 1, "pe")
                for i in range(TILES):
                    r = ROWS[i]
                    for ch in range(3):
                        w = 128 if ch < 2 else 64
                        pe.transpose(bank[2 * i][0:w, ch * P:ch * P + r], proj[0:r, i, XB0 + ch * P:XB0 + ch * P + w], ident[0:r, 0:r])
                        last = pe.transpose(bank[2 * i + 1][0:w, ch * P:ch * P + r], proj[0:r, i, GB0 + ch * P:GB0 + ch * P + w], ident[0:r, 0:r])
                    last.then_inc(zg_ps, 1)
                hold(pe, qkv_done, l + 1, "pe")
                hold(pe, wmt_done, l + 1, "pe")
                for i in range(TILES):
                    r = ROWS[i]
                    if i == 2:
                        hold(pe, cblock_loaded, 256 * (l + 1), "pe")
                        hold(pe, yc_done, 3 * l + 1, "pe")
                    wt = wmt if i < 2 else wss
                    for h in range(CH):
                        last = pe.matmul(bank[6 + i % 2][0:r, h * HD:h * HD + HD], wt[0:r, h, 0:r],
                                         proj[0:r, i, CV0 + h * HD:CV0 + h * HD + HD], start=True, stop=True)
                    last.then_inc(mix_ps, 1)
                for i in range(TILES):
                    r = ROWS[i]
                    hold(pe, zg_done, 3 * l + i + 1, "pe")
                    hold(pe, yc_done, 3 * l + i + 1, "pe")
                    for ch in range(3):
                        last = pe.transpose(bank[2 * i][:, ch * P:ch * P + r], ycm[0:r, i, ch * P:ch * P + P], ident[0:r, 0:r])
                    last.then_inc(yct_ps, 1)
                for j in range(2 * TILES):
                    i = j // 2
                    r = ROWS[i]
                    if j >= 4:
                        hold(pe, qkt_done, 6 * l + j - 3, "pe")
                    for g in range(NG):
                        c0 = (K0 if j % 2 else Q0) + g * P
                        last = pe.transpose(bank[1 + 2 * (j % 4)][:, g * P:g * P + r], proj[0:r, i, c0:c0 + P], ident[0:r, 0:r])
                    last.then_inc(qkt_ps, 1)
                hold(pe, qkt_done, 6 * l + 6, "pe")
                hold(pe, yct_done, 3 * l + 3, "pe")

                def logits(q):
                    n = P * (q + 1)
                    for heads, b in lg_ps[q]:
                        for j, h in enumerate(heads):
                            r = slice(64 * (h % 2), 64 * (h % 2) + 64)
                            last = pe.matmul(b[:, n * j:n * j + n], qt[r, h // 2, q * P:q * P + P], kt[r, h // 2, 0:n],
                                             start=True, stop=True)
                    last.then_inc(logit_ps, 1)

                hold(pe, kq_summed, l + 1, "pe")
                for h in range(HEADS):
                    pe.transpose(old_ps[h // 3][:, h % 3, :], lgt[:, h, :], ident)
                for h in range(HEADS):
                    r = slice(64 * (h % 2), 64 * (h % 2) + 64)
                    last = pe.matmul(new_ps[h % 2][:, h // 2, :], qt[r, h // 2, SEQ:TOKENS], kt[r, h // 2, SEQ:TOKENS],
                                     start=True, stop=True)
                last.then_inc(logit_ps, 1)
                logits(1)
                hold(pe, max_done, 3 * l + 1, "pe")
                logits(0)
                hold(pe, prob_done, 3 * l + 1, "pe")
                for h in range(HEADS):
                    pe.transpose(pts_ps[:, h, :], lgs[0:NS, h, 0:P], ident[0:NS, 0:NS])
                    last = pe.transpose(pte_ps[0:NS, h, :], lgs[0:NS, h, P:P + NS], ident[0:NS, 0:NS])
                last.then_inc(probt_ps, 1)
                hold(pe, probt_done, 3 * l + 1, "pe")
                for h in range(HEADS):
                    r = slice(64 * (h % 2), 64 * (h % 2) + 64)
                    last = pe.matmul(pnew_sum[r, h // 2, :], proj[0:NS, 2, V0 + h * HD:V0 + h * HD + HD], pte[0:NS, h, :],
                                     start=True, stop=True)
                last.then_inc(pnew_ps, 1)
                for slot, q, rows in ((1, 1, (2, 3, 0, 1)), (2, 0, (4, 5, 6, 7))):
                    for b in rows:
                        hold(pe, cache_in[b], 304 * (l + 1) if b < 2 else 48 * (l + 1), "pe")
                        r = slice(b * NT, b * NT + NT)
                        last = pe.matmul(pv_sum[:, 0, :, r], cval[b][2], pts[:, 0:2, r], start=True, stop=True)
                        for t in range(NT):
                            for g in (1, 2):
                                n = b * NT + t
                                last = pe.matmul(pv_sum[:, g, :, n], cval[b][g - 1][:, t, :], pts[:, 2 * g:2 * g + 2, n], start=True, stop=True)
                    if slot == 2:
                        last.then_inc(pv_done, 1)
                    hold(pe, prob_done, 3 * l + slot + 1, "pe")
                    for h in range(HEADS):
                        for kb in range(q + 1):
                            j = h * (q + 1) + kb
                            last = pe.transpose(prob_banks[q][j // 4][:, (j % 4) * P:(j % 4 + 1) * P], lgp[:, q, h, kb * P:kb * P + P], ident)
                    last.then_inc(probt_ps, 1)
                    hold(pe, probt_done, 3 * l + slot + 1, "pe")
                    for h in range(HEADS):
                        r = slice(64 * (h % 2), 64 * (h % 2) + 64)
                        for kb in range(q + 1):
                            j = h * (q + 1) + kb
                            last = pe.matmul(ya_bank[q][r, (h // 2) * P:(h // 2 + 1) * P], proj[:, kb, V0 + h * HD:V0 + h * HD + HD],
                                             (pt0 if q == 0 else pt1)[:, j, :], start=(kb == 0), stop=(kb == q))
                    last.then_inc(ya_ps, 1)
                hold(pe, ya_done, 2 * l + 2, "pe")
                hold(pe, yas_done, l + 1, "pe")
                hold(pe, yb_done, l + 1, "pe")
                with pe.Fori(0, N_OUT // 2) as c:
                    for s in range(2):
                        w = wring[:, s, 0:KCH * W_OUT].rearrange("p (k n) -> p k n", k=KCH)
                        hold(pe, w_loaded[s], 16 * (N_W // 2 * l + N_IN // 2 + c + 1), "pe")
                        for i in range(TILES):
                            hold(pe, h_done, 12 * l + 6 * c + 3 * s + i + 7, "pe")
                            for k in range(KCH):
                                last = pe.matmul(bank[3 * s + i][0:ROWS[i], 0:W_OUT], yt[:, k, T0[i]:T0[i] + ROWS[i]], w[:, k, :],
                                                 start=(k == 0), stop=(k == KCH - 1))
                            last.then_inc(h_ps, 1)
                norm_t(l, 1)
                hold(pe, keys_loaded, 32 * (l + 1), "pe")
                for j in range(2):
                    last = pe.transpose(bank[6][:, j * P:j * P + P], kraw[:, j, :], ident)
                last.then_inc(keyt_ps, 1)
                def queries(lo, hi):
                    with pe.Fori(lo, hi) as c:
                        for s in range(2):
                            w = wring[:, s, 0:KCH * W_Q].rearrange("p (k n) -> p k n", k=KCH)
                            hold(pe, w_loaded[s], 16 * (N_W // 2 * l + (N_IN + N_OUT) // 2 + c + 1), "pe")
                            for j in range(2):
                                hold(pe, qf_done, 16 * l + 4 * c + 2 * s + j + 1, "pe")
                                for k in range(KCH):
                                    last = pe.matmul(bank[2 * s + j][:, 0:TOKENS], w[:, k, j * P:j * P + P], xt[:, k, :],
                                                     start=(k == 0), stop=(k == KCH - 1))
                                last.then_inc(qf_ps, 1)

                queries(0, 1)
                hold(pe, keyt_done, l + 1, "pe")
                hold(pe, qf_done, 16 * l + 8, "pe")
                score(l, 0)
                queries(1, 2)
                hold(pe, qf_done, 16 * l + 12, "pe")
                score(l, 1)
                queries(2, 4)
                hold(pe, qf_done, 16 * l + 20, "pe")
                score(l, 2)
                hold(pe, score_done, NP * l + 3, "pe")
                score(l, 3)
                score(l, 4)
                open_y(l, 0)
                batches(l, 0, 0, 6)
                hold(pe, score_done, NP * l + 5, "pe")
                score(l, 5)
                score(l, 6)
                batches(l, 0, 6, 16)
                close_y(l, 0)
                open_y(l, 1)
                batches(l, 1, 0, 16)
                close_y(l, 1)
                open_y(l, 2)
                batches(l, 2, 0, 4)
                close_y(l, 2)


_INS = ("x_prompt", "x_sample", "cache_a_kv_w128", "cache_a_kv_w512", "cache_a_kv_w2048", "state_b_conv", "rel_bias",
        "norm_mix", "w_in", "q_norm", "k_norm", "conv_w", "c_v_norm", "c_ws", "c_bs", "w_out", "norm_ffn", "peer_wq",
        "peer_k1", "peer_k2", "peer_u", "peer_v")
_OUTS = (("y_prompt", (1, SEQ, D)), ("y_sample", (NB, NT, D)),
         ("kvp128", (DEPTH, 1, 128, 2, 2, HD)), ("kvs128", (DEPTH, NB, 128, 2, 2, HD)),
         ("kvp512", (DEPTH, 1, SEQ, 2, 2, HD)), ("kvs512", (DEPTH, NB, 512, 2, 2, HD)),
         ("kvp2048", (DEPTH, 1, SEQ, 2, 2, HD)), ("kvs2048", (DEPTH, NB, 2048, 2, 2, HD)),
         ("conv_prompt", (DEPTH, 1, 2, BW)), ("conv_sample", (DEPTH, NB, 2, BW)),
         ("chunk_v", (DEPTH, NB, NT, CH, HD)))


def kernel(**inputs):
    import concourse.bacc as bacc
    from concourse.bass_utils import run_bass_kernel_spmd as run

    nc = bacc.Bacc("TRN2", target_bir_lowering=False, num_devices=1)
    arrays = {name: np.ascontiguousarray(inputs[name]) for name in _INS}
    arrays.update(shape_constants())
    io = {name: nc.dram_tensor(name, a.shape, F32, kind="ExternalInput").ap() for name, a in arrays.items()}
    for name, shape in _OUTS:
        io[name] = nc.dram_tensor(name, shape, F32, kind="ExternalOutput").ap()
    trunk(nc, io)
    got = run(nc, [arrays], core_ids=[0]).results[0]
    return tuple(got[name] for name, _ in _OUTS)
```
